# Optimizing a Trainium2 kernel written in Bass

```python
import jax, jax.numpy as jnp
from jax import lax
import numpy as np
import math

D_MODEL = 2048
BATCH = 1
SEQ = 256
DEPTH = 2

D_MIX = D_MODEL
EPS = 1e-6
SWA_HEAD_DIM = 64
SWA_HEADS = D_MIX // 2 // SWA_HEAD_DIM
SWA_KV_HEADS = 4
SWA_GROUP = SWA_HEADS // SWA_KV_HEADS
SWA_WIDTH = SWA_HEADS * SWA_HEAD_DIM
SWA_KV_WIDTH = SWA_KV_HEADS * SWA_HEAD_DIM
WINDOW = 128
ROT_DIM = SWA_HEAD_DIM // 4
ROPE_THETA = 500000.0
SG_WIDTH = D_MIX // 4
SG_GROUPS = 8
SG_GROUP_DIM = SG_WIDTH // SG_GROUPS
SG_CHUNK = 128
GLA_HEADS = 4
GLA_WIDTH = D_MIX // 4
GLA_DV = GLA_WIDTH // GLA_HEADS
GLA_DK = GLA_DV // 2
GLA_KEY_WIDTH = GLA_HEADS * GLA_DK
GLA_GATE_RANK = 16
GLA_GATE_TAU = 16.0
GLA_CHUNK = 64
IN_SIZES = (SWA_WIDTH, SWA_KV_WIDTH, SWA_KV_WIDTH,
            SG_WIDTH, SG_WIDTH,
            GLA_KEY_WIDTH, GLA_KEY_WIDTH, GLA_WIDTH,
            GLA_GATE_RANK,
            D_MIX)
IN_PROJ_WIDTH = SWA_WIDTH + 2 * SWA_KV_WIDTH + 2 * SG_WIDTH + 2 * GLA_KEY_WIDTH + GLA_WIDTH + GLA_GATE_RANK + D_MIX


def rms_norm(x, g):
    x32 = x.astype(jnp.float32)
    y = x32 * lax.rsqrt(jnp.mean(x32 * x32, axis=-1, keepdims=True) + EPS)
    return (y * g.astype(jnp.float32)).astype(x.dtype)

def partial_rope(t, positions):
    half = ROT_DIM // 2
    inv_freq = ROPE_THETA ** (-(jnp.arange(half, dtype=jnp.float32) * (2.0 / ROT_DIM)))
    ang = positions.astype(jnp.float32)[..., None] * inv_freq
    cos = jnp.cos(ang)[:, :, None, :]
    sin = jnp.sin(ang)[:, :, None, :]
    tr = t[..., :ROT_DIM].astype(jnp.float32)
    t1, t2 = tr[..., :half], tr[..., half:]
    rot = jnp.concatenate([t1 * cos - t2 * sin, t2 * cos + t1 * sin], axis=-1)
    return jnp.concatenate([rot.astype(t.dtype), t[..., ROT_DIM:]], axis=-1)

def sliding_window_attention(q, k, v, sinks):
    bsz, seq = q.shape[0], q.shape[1]
    nb = seq // WINDOW
    qb = q.reshape(bsz, nb, WINDOW, SWA_KV_HEADS, SWA_GROUP, SWA_HEAD_DIM).astype(jnp.float32)

    def band(t):
        tb = t.reshape(bsz, nb, WINDOW, SWA_KV_HEADS, SWA_HEAD_DIM)
        prev = jnp.pad(tb[:, :-1], ((0, 0), (1, 0), (0, 0), (0, 0), (0, 0)))
        return jnp.concatenate([prev, tb], axis=2).astype(jnp.float32)

    kb, vb = band(k), band(v)
    scores = jnp.einsum('bnqgrd,bnkgd->bngrqk', qb, kb) * (SWA_HEAD_DIM ** -0.5)
    qi = jnp.arange(WINDOW)[:, None]
    kj = jnp.arange(2 * WINDOW)[None, :]
    dist = qi + WINDOW - kj
    blk = jnp.arange(nb)[:, None, None]
    valid = (dist >= 0) & (dist < WINDOW) & (blk * WINDOW + kj[None] - WINDOW >= 0)
    scores = jnp.where(valid[None, :, None, None], scores, -jnp.inf)
    sink = sinks.astype(jnp.float32).reshape(1, 1, SWA_KV_HEADS, SWA_GROUP, 1, 1)
    m = jnp.maximum(scores.max(axis=-1, keepdims=True), sink)
    p = jnp.exp(scores - m)
    probs = p / (p.sum(axis=-1, keepdims=True) + jnp.exp(sink - m))
    out = jnp.einsum('bngrqk,bnkgd->bnqgrd', probs, vb)
    return out.reshape(bsz, seq, SWA_WIDTH).astype(q.dtype)

def chunked_spatial_gating(u, v, w_s, b_s, ln_g, ln_b):
    bsz, seq = v.shape[0], v.shape[1]
    nc = seq // SG_CHUNK
    v32 = v.astype(jnp.float32)
    mu = jnp.mean(v32, axis=-1, keepdims=True)
    var = jnp.mean(jnp.square(v32 - mu), axis=-1, keepdims=True)
    vn = (v32 - mu) * lax.rsqrt(var + EPS) * ln_g.astype(jnp.float32) + ln_b.astype(jnp.float32)
    vn = vn.reshape(bsz, nc, SG_CHUNK, SG_GROUPS, SG_GROUP_DIM)
    causal = jnp.tril(jnp.ones((SG_CHUNK, SG_CHUNK), dtype=bool))
    w = jnp.where(causal[None], w_s.astype(jnp.float32), 0.0)
    mixed = jnp.einsum('gts,bnsgc->bntgc', w, vn) + b_s.astype(jnp.float32).T[None, None, :, :, None]
    return (u.astype(jnp.float32) * mixed.reshape(bsz, seq, SG_WIDTH)).astype(u.dtype)

def gated_linear_attention(q, k, v, log_alpha):
    bsz, seq = q.shape[0], q.shape[1]
    nc = seq // GLA_CHUNK

    def to_chunks(t):
        return t.astype(jnp.float32).reshape(bsz, nc, GLA_CHUNK, GLA_HEADS, t.shape[-1]).transpose(1, 0, 3, 2, 4)

    causal = jnp.tril(jnp.ones((GLA_CHUNK, GLA_CHUNK), dtype=bool))

    def step(state, xs):
        qc, kc, vc, lac = xs
        b = jnp.cumsum(lac, axis=2)
        diff = b[:, :, :, None, :] - b[:, :, None, :, :]
        decay = jnp.exp(jnp.where(causal[:, :, None], diff, -jnp.inf))
        scores = jnp.einsum('bhtd,bhsd,bhtsd->bhts', qc, kc, decay)
        o = jnp.einsum('bhts,bhsv->bhtv', scores, vc) + jnp.einsum('bhtd,bhdv->bhtv', qc * jnp.exp(b), state)
        b_last = b[:, :, -1:, :]
        state = state * jnp.exp(b_last)[:, :, 0, :, None] + jnp.einsum('bhsd,bhsv->bhdv', kc * jnp.exp(b_last - b), vc)
        return state, o

    state0 = jnp.zeros((bsz, GLA_HEADS, GLA_DK, GLA_DV), dtype=jnp.float32)
    qs = to_chunks(q) * (GLA_DK ** -0.5)
    _, o = lax.scan(step, state0, (qs, to_chunks(k), to_chunks(v), to_chunks(log_alpha)))
    return o.transpose(1, 0, 3, 2, 4).reshape(bsz, seq, GLA_HEADS, GLA_DV)

def hybrid_layer(x, c, positions, w_mod, b_mod, g_pre, g_post, w_in, w_out, swa_sinks,
                 sg_w, sg_b, sg_ln_g, sg_ln_b, gla_w_gate_up, gla_b_gate, gla_norm_g):
    bsz, seq = x.shape[0], x.shape[1]
    mod = jax.nn.silu(c) @ w_mod + b_mod
    shift, scale, gate = jnp.split(mod, 3, axis=-1)
    h = rms_norm(x, g_pre) * (1.0 + scale[:, None, :]) + shift[:, None, :]
    proj = h @ w_in
    offsets = np.cumsum(IN_SIZES)[:-1].tolist()
    a_q, a_k, a_v, s_u, s_v, c_q, c_k, c_v, c_g, z = jnp.split(proj, offsets, axis=-1)
    a_q = partial_rope(a_q.reshape(bsz, seq, SWA_HEADS, SWA_HEAD_DIM), positions)
    a_k = partial_rope(a_k.reshape(bsz, seq, SWA_KV_HEADS, SWA_HEAD_DIM), positions)
    a_v = a_v.reshape(bsz, seq, SWA_KV_HEADS, SWA_HEAD_DIM)
    y_a = sliding_window_attention(a_q, a_k, a_v, swa_sinks)
    y_b = chunked_spatial_gating(jax.nn.gelu(s_u), jax.nn.gelu(s_v), sg_w, sg_b, sg_ln_g, sg_ln_b)
    gate_logits = (c_g @ gla_w_gate_up + gla_b_gate).astype(jnp.float32)
    log_alpha = jax.nn.log_sigmoid(gate_logits) / GLA_GATE_TAU
    o_c = gated_linear_attention(c_q.reshape(bsz, seq, GLA_HEADS, GLA_DK),
                                 c_k.reshape(bsz, seq, GLA_HEADS, GLA_DK),
                                 c_v.reshape(bsz, seq, GLA_HEADS, GLA_DV),
                                 log_alpha.reshape(bsz, seq, GLA_HEADS, GLA_DK))
    y_c = rms_norm(o_c, gla_norm_g).reshape(bsz, seq, GLA_WIDTH).astype(x.dtype)
    y = jnp.concatenate([y_a, y_b, y_c], axis=-1) * jax.nn.silu(z)
    out = y @ w_out
    return x + gate[:, None, :] * rms_norm(out, g_post)

def first_inputs(seed: int = 0) -> dict:
    key = jax.random.key(seed)
    ks = jax.random.split(key, 17)
    nrm = jax.random.normal
    f32 = jnp.float32
    x = nrm(ks[0], (BATCH, SEQ, D_MODEL), f32)
    c = nrm(ks[1], (BATCH, D_MODEL), f32)
    positions = jax.random.randint(ks[2], (BATCH, 1), 0, 4096, dtype=jnp.int32) + jnp.arange(SEQ, dtype=jnp.int32)[None, :]
    w_mod = nrm(ks[3], (DEPTH, D_MODEL, 3 * D_MODEL), f32) * (0.5 * D_MODEL ** -0.5)
    b_mod = 0.01 * nrm(ks[4], (DEPTH, 3 * D_MODEL), f32)
    g_pre = 1.0 + 0.05 * nrm(ks[5], (DEPTH, D_MODEL), f32)
    g_post = 1.0 + 0.05 * nrm(ks[6], (DEPTH, D_MODEL), f32)
    w_in = nrm(ks[7], (DEPTH, D_MODEL, IN_PROJ_WIDTH), f32) * (D_MODEL ** -0.5)
    w_out = nrm(ks[8], (DEPTH, D_MIX, D_MODEL), f32) * (D_MIX ** -0.5)
    swa_sinks = 0.5 * nrm(ks[9], (DEPTH, SWA_HEADS), f32)
    sg_w = nrm(ks[10], (DEPTH, SG_GROUPS, SG_CHUNK, SG_CHUNK), f32) * (SG_CHUNK ** -0.5)
    sg_b = 1.0 + 0.1 * nrm(ks[11], (DEPTH, SG_GROUPS, SG_CHUNK), f32)
    sg_ln_g = 1.0 + 0.05 * nrm(ks[12], (DEPTH, SG_WIDTH), f32)
    sg_ln_b = 0.02 * nrm(ks[13], (DEPTH, SG_WIDTH), f32)
    gla_w_gate_up = nrm(ks[14], (DEPTH, GLA_GATE_RANK, GLA_KEY_WIDTH), f32) * (GLA_GATE_RANK ** -0.5)
    gla_b_gate = 0.1 * nrm(ks[15], (DEPTH, GLA_KEY_WIDTH), f32)
    gla_norm_g = 1.0 + 0.05 * nrm(ks[16], (DEPTH, GLA_DV), f32)
    return {'x': x, 'c': c, 'positions': positions, 'w_mod': w_mod, 'b_mod': b_mod,
            'g_pre': g_pre, 'g_post': g_post, 'w_in': w_in, 'w_out': w_out, 'swa_sinks': swa_sinks,
            'sg_w': sg_w, 'sg_b': sg_b, 'sg_ln_g': sg_ln_g, 'sg_ln_b': sg_ln_b,
            'gla_w_gate_up': gla_w_gate_up, 'gla_b_gate': gla_b_gate, 'gla_norm_g': gla_norm_g}

def first_block(x, c, positions, w_mod, b_mod, g_pre, g_post, w_in, w_out, swa_sinks,
              sg_w, sg_b, sg_ln_g, sg_ln_b, gla_w_gate_up, gla_b_gate, gla_norm_g):
    for l in range(DEPTH):
        x = hybrid_layer(x, c, positions, w_mod[l], b_mod[l], g_pre[l], g_post[l], w_in[l], w_out[l],
                         swa_sinks[l], sg_w[l], sg_b[l], sg_ln_g[l], sg_ln_b[l],
                         gla_w_gate_up[l], gla_b_gate[l], gla_norm_g[l])
    return x


CHUNK = 64
Q_BLOCK = 128
HA = 8
A_NOPE = 128
A_ROPE = 64
A_V = 128
Q_RANK = 384
KV_RANK = 128
ROPE_THETA_2 = 10000.0
HB = 4
B_DH = 64
HC = 4
C_DH = 128
LEFT_CHUNKS = 8
REL_CLIP = 256
REL_SIZE = REL_CLIP + CHUNK
MIX_WIDTH = HA * A_V + HB * 2 * B_DH + HC * C_DH
IN_SIZES_2 = (Q_RANK, KV_RANK, A_ROPE,
            HB * 2 * B_DH, HB * 2 * B_DH, HB * 2 * B_DH,
            HC * C_DH, HC * C_DH, HC * C_DH)
IN_WIDTH = sum(IN_SIZES_2)
D_FF = 4 * D_MODEL
NEG = -1e30


def rms_norm_2(x, g):
    xf = x.astype(jnp.float32)
    y = xf * lax.rsqrt(jnp.mean(xf * xf, axis=-1, keepdims=True) + EPS)
    return (y * g.astype(jnp.float32)).astype(x.dtype)

def apply_rope(x, pos):
    half = x.shape[-1] // 2
    inv_freq = ROPE_THETA_2 ** (-jnp.arange(half, dtype=jnp.float32) / half)
    ang = pos.astype(jnp.float32)[:, None] * inv_freq[None, :]
    cos = jnp.cos(ang)[:, None, :]
    sin = jnp.sin(ang)[:, None, :]
    xf = x.astype(jnp.float32)
    x1, x2 = xf[..., :half], xf[..., half:]
    return jnp.concatenate([x1 * cos - x2 * sin, x2 * cos + x1 * sin], axis=-1).astype(x.dtype)

def chunk_causal_mask(q_pos, seq):
    k_chunk = jnp.arange(seq) // CHUNK
    return k_chunk[None, :] <= (q_pos // CHUNK)[:, None]

def sweep_query_blocks(block_fn, q):
    b, h, s = q.shape[:3]
    nblk = s // Q_BLOCK
    qb = jnp.moveaxis(q.reshape((b, h, nblk, Q_BLOCK) + q.shape[3:]), 2, 0)
    out = lax.map(lambda a: block_fn(a[0], a[1]), (qb, jnp.arange(nblk)))
    return out.transpose(1, 0, 3, 2, 4).reshape(b, s, h * out.shape[-1])

def mla_mixer(c_q, c_kv, k_rope, q_norm, kv_norm, w_uq, w_ukv):
    b, s, _ = c_q.shape
    pos = jnp.arange(s)
    q = (rms_norm_2(c_q, q_norm) @ w_uq).reshape(b, s, HA, A_NOPE + A_ROPE)
    q = jnp.concatenate([q[..., :A_NOPE], apply_rope(q[..., A_NOPE:], pos)], axis=-1)
    kv = (rms_norm_2(c_kv, kv_norm) @ w_ukv).reshape(b, s, HA, A_NOPE + A_V)
    kr = apply_rope(k_rope[:, :, None, :], pos)
    k = jnp.concatenate([kv[..., :A_NOPE], jnp.broadcast_to(kr, (b, s, HA, A_ROPE))], axis=-1)
    q = q.transpose(0, 2, 1, 3)
    k = k.transpose(0, 2, 1, 3)
    v = kv[..., A_NOPE:].transpose(0, 2, 1, 3)
    scale = (A_NOPE + A_ROPE) ** -0.5

    def block(qb, blk):
        q_pos = blk * Q_BLOCK + jnp.arange(Q_BLOCK)
        sc = jnp.einsum('bhqd,bhkd->bhqk', qb, k).astype(jnp.float32) * scale
        sc = jnp.where(chunk_causal_mask(q_pos, s), sc, NEG)
        p = jax.nn.softmax(sc, axis=-1).astype(v.dtype)
        return jnp.einsum('bhqk,bhkd->bhqd', p, v)

    return sweep_query_blocks(block, q)

def diff_mixer(q, k, v, lq1, lk1, lq2, lk2, subln, lam_init):
    b, s, _ = q.shape
    q = q.reshape(b, s, HB, 2, B_DH).transpose(0, 2, 1, 3, 4)
    k = k.reshape(b, s, HB, 2, B_DH).transpose(0, 2, 1, 3, 4)
    v = v.reshape(b, s, HB, 2 * B_DH).transpose(0, 2, 1, 3)
    f32 = jnp.float32
    lam = (jnp.exp(jnp.sum(lq1.astype(f32) * lk1.astype(f32)))
           - jnp.exp(jnp.sum(lq2.astype(f32) * lk2.astype(f32))) + lam_init)
    slopes = 2.0 ** (-8.0 * (jnp.arange(HB, dtype=f32) + 1.0) / HB)
    k_pos = jnp.arange(s)
    scale = B_DH ** -0.5

    def block(qb, blk):
        q_pos = blk * Q_BLOCK + jnp.arange(Q_BLOCK)
        sc = jnp.einsum('bhqnd,bhknd->nbhqk', qb, k).astype(f32) * scale
        dist = jnp.abs(q_pos[:, None] - k_pos[None, :]).astype(f32)
        sc = sc - slopes[:, None, None] * dist
        sc = jnp.where(chunk_causal_mask(q_pos, s), sc, NEG)
        p = jax.nn.softmax(sc, axis=-1)
        w = (p[0] - lam * p[1]).astype(v.dtype)
        o = jnp.einsum('bhqk,bhkd->bhqd', w, v)
        return rms_norm_2(o, subln) * (1.0 - lam_init)

    return sweep_query_blocks(block, q)

def chunk_band_mixer(q, k, v, rel_bias):
    b, s, _ = q.shape
    nc = s // CHUNK
    win = LEFT_CHUNKS + 1
    idx = jnp.arange(nc)[:, None] + jnp.arange(win)[None, :]

    def band(t):
        t = t.reshape(b, nc, CHUNK, HC, C_DH)
        t = jnp.pad(t, ((0, 0), (LEFT_CHUNKS, 0), (0, 0), (0, 0), (0, 0)))
        return t[:, idx].reshape(b, nc, win * CHUNK, HC, C_DH)

    qc = q.reshape(b, nc, CHUNK, HC, C_DH)
    kb, vb = band(k), band(v)
    valid = (jnp.arange(nc)[:, None] - LEFT_CHUNKS + jnp.arange(win)[None, :]) >= 0
    valid = jnp.repeat(valid, CHUNK, axis=1)
    rel = LEFT_CHUNKS * CHUNK + jnp.arange(CHUNK)[:, None] - jnp.arange(win * CHUNK)[None, :]
    rel_idx = jnp.clip(rel, -(CHUNK - 1), REL_CLIP) + (CHUNK - 1)
    bias = rel_bias[:, rel_idx].astype(jnp.float32)
    sc = jnp.einsum('bcqhd,bckhd->bchqk', qc, kb).astype(jnp.float32) * (C_DH ** -0.5)
    sc = sc + bias[None, None]
    sc = jnp.where(valid[None, :, None, None, :], sc, NEG)
    p = jax.nn.softmax(sc, axis=-1).astype(vb.dtype)
    o = jnp.einsum('bchqk,bckhd->bcqhd', p, vb)
    return o.reshape(b, s, HC * C_DH)

def second_inputs(seed: int = 0) -> dict:
    key = jax.random.key(seed)
    ks = jax.random.split(key, 20)
    f32 = jnp.float32
    nrm = lambda k, shape, s: jax.random.normal(k, shape, f32) * s
    gain = lambda k, shape: 1.0 + 0.02 * jax.random.normal(k, shape, f32)
    return {
        "x": nrm(ks[0], (BATCH, SEQ, D_MODEL), 1.0),
        "attn_norm": gain(ks[1], (DEPTH, D_MODEL)),
        "w_in": nrm(ks[2], (DEPTH, D_MODEL, IN_WIDTH), D_MODEL ** -0.5),
        "q_a_norm": gain(ks[3], (DEPTH, Q_RANK)),
        "kv_a_norm": gain(ks[4], (DEPTH, KV_RANK)),
        "w_uq": nrm(ks[5], (DEPTH, Q_RANK, HA * (A_NOPE + A_ROPE)), Q_RANK ** -0.5),
        "w_ukv": nrm(ks[6], (DEPTH, KV_RANK, HA * (A_NOPE + A_V)), KV_RANK ** -0.5),
        "lambda_q1": nrm(ks[7], (DEPTH, B_DH), 0.1),
        "lambda_k1": nrm(ks[8], (DEPTH, B_DH), 0.1),
        "lambda_q2": nrm(ks[9], (DEPTH, B_DH), 0.1),
        "lambda_k2": nrm(ks[10], (DEPTH, B_DH), 0.1),
        "diff_subln": gain(ks[11], (DEPTH, 2 * B_DH)),
        "rel_bias": nrm(ks[12], (DEPTH, HC, REL_SIZE), 0.1),
        "w_o": nrm(ks[13], (DEPTH, MIX_WIDTH, D_MODEL), MIX_WIDTH ** -0.5),
        "mlp_norm": gain(ks[14], (DEPTH, D_MODEL)),
        "w_up": nrm(ks[15], (DEPTH, D_MODEL, D_FF), D_MODEL ** -0.5),
        "w_down": nrm(ks[16], (DEPTH, D_FF, D_MODEL), D_FF ** -0.5),
        "final_norm": gain(ks[17], (D_MODEL,)),
    }

def second_block(x, attn_norm, w_in, q_a_norm, kv_a_norm, w_uq, w_ukv,
              lambda_q1, lambda_k1, lambda_q2, lambda_k2, diff_subln, rel_bias,
              w_o, mlp_norm, w_up, w_down, final_norm):
    split_points = np.cumsum(np.array(IN_SIZES_2))[:-1]
    for l in range(DEPTH):
        h = rms_norm_2(x, attn_norm[l])
        proj = h @ w_in[l]
        (c_q, c_kv, k_rope, qb, kb, vb, qc, kc, vc) = jnp.split(proj, split_points, axis=-1)
        out_a = mla_mixer(c_q, c_kv, k_rope, q_a_norm[l], kv_a_norm[l], w_uq[l], w_ukv[l])
        lam_init = 0.8 - 0.6 * math.exp(-0.3 * l)
        out_b = diff_mixer(qb, kb, vb, lambda_q1[l], lambda_k1[l], lambda_q2[l],
                           lambda_k2[l], diff_subln[l], lam_init)
        out_c = chunk_band_mixer(qc, kc, vc, rel_bias[l])
        mixed = jnp.concatenate([out_a, out_b, out_c], axis=-1)
        x = x + mixed @ w_o[l]
        h = rms_norm_2(x, mlp_norm[l])
        x = x + jnp.square(jax.nn.relu(h @ w_up[l])) @ w_down[l]
    return rms_norm_2(x, final_norm)


def setup_inputs(seed=0):
    out = dict(first_inputs(seed))
    for name, value in second_inputs(seed + 1).items():
        if name != "x":
            out[name + "_2"] = value
    return out


def reference(
    x, c, positions, w_mod, b_mod, g_pre, g_post, w_in, w_out, swa_sinks, sg_w, sg_b, sg_ln_g,
    sg_ln_b, gla_w_gate_up, gla_b_gate, gla_norm_g, attn_norm_2, w_in_2, q_a_norm_2,
    kv_a_norm_2, w_uq_2, w_ukv_2, lambda_q1_2, lambda_k1_2, lambda_q2_2, lambda_k2_2,
    diff_subln_2, rel_bias_2, w_o_2, mlp_norm_2, w_up_2, w_down_2, final_norm_2,
):
    x = first_block(
        x, c, positions, w_mod, b_mod, g_pre, g_post, w_in, w_out, swa_sinks, sg_w, sg_b,
        sg_ln_g, sg_ln_b, gla_w_gate_up, gla_b_gate, gla_norm_g,
    )
    return second_block(
        x, attn_norm_2, w_in_2, q_a_norm_2, kv_a_norm_2, w_uq_2, w_ukv_2, lambda_q1_2,
        lambda_k1_2, lambda_q2_2, lambda_k2_2, diff_subln_2, rel_bias_2, w_o_2, mlp_norm_2,
        w_up_2, w_down_2, final_norm_2,
    )


_drawn_inputs = setup_inputs


def setup_inputs(seed=0):
    import zlib

    import numpy as np

    out = dict(_drawn_inputs(seed))
    spreads = {}
    factors = {'swa_sinks': 7.861,
     'sg_ln_g': 6.328,
     'sg_ln_b': 8.0,
     'gla_b_gate': 3.141,
     'gla_norm_g': 2.973,
     'attn_norm_2': 3.655,
     'q_a_norm_2': 8.0,
     'kv_a_norm_2': 8.0,
     'lambda_q1_2': 7.929,
     'lambda_q2_2': 3.064,
     'lambda_k2_2': 3.648,
     'diff_subln_2': 5.616,
     'rel_bias_2': 7.268,
     'final_norm_2': 2.797}
    for name, (base, spread) in spreads.items():
        noise = np.random.default_rng([zlib.crc32(name.encode()), seed]).standard_normal(out[name].shape)
        drawn = base * np.exp(spread * noise) if base else spread * noise
        out[name] = __import__('jax').numpy.asarray(drawn.astype(out[name].dtype))
    for name, factor in factors.items():
        out[name] = (out[name] * factor).astype(out[name].dtype)
    return out
```

```python
from contextlib import ExitStack
import math

import numpy as np

import concourse.bass as bass
from concourse import mybir

F32 = mybir.dt.float32
F32R = mybir.dt.float32r
I32 = mybir.dt.int32
ACT = mybir.ActivationFunctionType
ALU = mybir.AluOpType
AX = mybir.AxisListType

P = 128
TOK = 2
D = 2048
KC = D // P
DEPTH = 2
EPS = 1e-6
BIG = 1e30
RAW_SLOTS = 8
SPLIT_SLOTS = 4
GROUP = 1024
COLS = 512

HD = 64
QH, KVH = 16, 4
C_Q, C_K, C_V, C_SU, C_SV, C_CQ, C_CK, C_CV, C_CG, C_Z = 0, 1024, 1280, 1536, 2048, 2560, 2816, 3072, 3584, 3600
W1 = 5648
SGG, SGD = 8, 64
GH, GDK, GDV, RANK = 4, 64, 128, 16
LEVELS = 7
HALF = 8
C_CQ2, C_CKV, C_KR, C_QB, C_KB, C_VB, C_QC, C_KC, C_VC = 0, 384, 512, 576, 1088, 1600, 2112, 2624, 3136
W2 = 3648
HA, NOPE, ROPE, VA = 8, 128, 64, 128
DFF = 4 * D
UPC = 4096
REL = 320
REL_PAD = 384

CONST_COLS = {}
ROUND = 1.5 * 2 ** 23
TWO_PI = (6.28125, 2029.0 / 2 ** 20, 2 * np.pi - 6.28125 - 2029.0 / 2 ** 20)
PI_BELOW = 3.1415925
_at = 0
for _name, _n in (("ident", 128), ("flip", 128), ("ones", 128), ("swa", 256), ("chunk", 256), ("tril", 128),
                  ("inv_freq", HALF), ("cos2", 64), ("sin2", 64)):
    CONST_COLS[_name] = (_at, _n)
    _at += _n
CONST_W = _at


def constants():
    q = np.arange(P)[:, None]
    k = np.arange(2 * P)[None, :]
    c = np.zeros((P, CONST_W), np.float32)

    def put(name, v):
        a, n = CONST_COLS[name]
        c[:, a:a + n] = v
    put("ident", np.eye(P))
    put("flip", np.eye(P)[::-1])
    put("ones", 1.0)
    dist = q + P - k
    put("swa", np.where((dist >= 0) & (dist < P), 0.0, -BIG))
    put("chunk", np.where(k // 64 <= (q + P) // 64, 0.0, -BIG))
    put("tril", (q <= np.arange(P)[None, :]))
    f1 = np.float32(500000.0) ** (-(np.arange(HALF, dtype=np.float32) * np.float32(2.0 / 16)))
    put("inv_freq", f1[None, :])
    f2 = np.float32(10000.0) ** (-np.arange(32, dtype=np.float32) / np.float32(32))
    ang = np.arange(2 * P, dtype=np.float32)[:, None] * f2[None, :]
    lay = lambda v: v.reshape(2, P, 32).transpose(1, 0, 2).reshape(P, 64)
    put("cos2", lay(np.cos(ang.astype(np.float64))))
    put("sin2", lay(np.sin(ang.astype(np.float64))))
    s = np.arange(P)[:, None]
    t = np.arange(P)[None, :]
    lv = [s == t]
    for n in range(1, LEVELS + 1):
        b = 2 ** n
        lv.append((s // b == t // b) & (s % b < b // 2) & (t % b >= b // 2))
    levels = np.concatenate([m.astype(np.int32) for m in lv], axis=1)
    slopes = (2.0 ** (-8.0 * (np.arange(4, dtype=np.float32) + 1.0) / 4)).astype(np.float32)
    d2 = np.abs(q + P - k).astype(np.float32)
    ok = k // 64 <= (q + P) // 64
    diff = np.concatenate([np.where(ok, -sl * d2, -BIG).astype(np.float32) for sl in slopes], axis=1)
    return c, levels, diff


class Tally:

    def __init__(self):
        self.n = {}

    def __call__(self, sem, by=1):
        self.n[sem.name] = self.n.get(sem.name, 0) + by
        return self.n[sem.name]

    def so_far(self, sem):
        return self.n.get(sem.name, 0)


class Job:

    def __init__(self, name, w, chunks, ncols, width, lhs, col0=0, lhs0=0, evac="act"):
        self.name, self.w, self.chunks, self.width, self.lhs = name, w, chunks, width, lhs
        self.tiles = ncols // width
        self.col0, self.lhs0, self.evac = col0, lhs0, evac
        per = max(1, GROUP // width) if width >= 256 else chunks
        self.groups = [(k, min(per, chunks - k)) for k in range(0, chunks, per)]


def build(nc, io):
    ctx = ExitStack()
    with ctx:
        cursor = [(nc.sbuf_base + 63) // 64 * 64]
        made = {}

        def at(name, shape, dt, offset):
            made[name] = nc.alloc_sbuf_tensor_at(name, shape, dt, offset=offset)
            return made[name]

        def words(shape):
            return int(np.prod(shape[1:]))

        def sb(name, shape, dt=F32):
            t = at(name, shape, dt, cursor[0])
            cursor[0] += (4 * words(shape) + 31) // 32 * 32
            return t

        class Area:

            def __init__(self, start):
                self.start = self.end = start

            def __call__(self, name, shape, dt=F32):
                t = at(name, shape, dt, self.end)
                self.end += (4 * words(shape) + 31) // 32 * 32
                return t

        x = sb("x", [P, TOK, D])
        hT_at = cursor[0]
        hT_hi = sb("hT_hi", [P, KC, 2 * P], F32R)
        hT_lo = sb("hT_lo", [P, KC, 2 * P], F32R)
        raw = sb("raw", [P, RAW_SLOTS, GROUP])
        w_hi = sb("w_hi", [P, SPLIT_SLOTS, GROUP], F32R)
        w_lo = sb("w_lo", [P, SPLIT_SLOTS, GROUP], F32R)
        hf = sb("hf", [P, 2, 2, 2 * P])
        cst = sb("cst", [P, CONST_W])
        K = {n: cst[:, a:a + w] for n, (a, w) in CONST_COLS.items()}
        ident = K["ident"]
        cols1 = sb("cols1", [P, DEPTH, 74])
        cols2 = sb("cols2", [P, DEPTH, 36])
        c_col = sb("c_col", [P, KC])
        minus_half = sb("minus_half", [P, 8])
        stat = sb("stat", [P, 64])
        cs1 = sb("cs1", [P, 2, TOK, HALF])
        turns = sb("turns", [P, TOK * HALF])
        bn = sb("bn", [P, TOK, 6])
        smax = sb("smax", [P, 2, 4])
        ssum = sb("ssum", [P, 2, 4])
        sden = sb("sden", [P, 2, 4])
        srec = sb("srec", [P, 2, 4])
        ses = sb("ses", [P, 2, 4])
        work_at = cursor[0]

        A1 = Area(work_at)
        proj = A1("proj", [P, TOK, W1])
        gp = A1("gp", [P, D])
        sinks = A1("sinks", [P, DEPTH, QH])
        neg_sinks = A1("neg_sinks", [P, DEPTH, QH])
        gnorm = A1("gnorm", [P, DEPTH, GDV])
        gup = A1("gup", [RANK, DEPTH, GH * GDK])
        hcol = A1("hcol", [P, 2, KC])
        A1g = Area(A1.end)
        acc = A1("acc", [P, 2, 2, COLS])
        gle = A1g("gle", [P, 2, 2, 2 * P])
        glf = A1g("glf", [P, 2, 2, 2 * P])
        levels = A1("levels", [P, LEVELS + 1, P], I32)
        probs = A1("probs", [P, 2, COLS])
        probsT = A1("probsT", [P, 2, COLS])
        glx = A1("glx", [P, 2, 2 * P])
        glb = A1("glb", [P, 2, 2 * P])
        cgT = A1("cgT", [RANK, 2 * P])
        A1h = Area(hT_at)
        q1T = A1h("q1T", [HD, QH, 2 * P])
        k1T = A1h("k1T", [HD, KVH, 2 * P])
        A1k = Area(hT_at)
        gq = A1k("gq", [P, 2, 2, 2 * P])
        qlev = A1k("qlev", [P, 2, 2, 2 * P])
        klev = A1k("klev", [P, 2, 2, 2 * P])
        pairs = A1k("pairs", [P, 3, COLS])
        sgw = A1h("sgw", [P, SGG, P])
        sgwT = A1h("sgwT", [P, SGG, P])
        sgln = A1h("sgln", [P, 2, COLS])
        modrow = proj
        xn = proj
        out_sb = proj
        oc = gle[:, :, :, :].rearrange("p a b n -> p (a b n)")
        osq = glf[:, :, :, :].rearrange("p a b n -> p (a b n)")

        A2 = Area(work_at)
        proj2 = A2("proj2", [P, TOK, W2])
        qm = A2("qm", [P, TOK, HA * (NOPE + ROPE)])
        kv = A2("kv", [P, TOK, HA * (NOPE + VA)])
        y2 = A2("y2", [P, TOK, D])
        probs2 = A2("probs2", [P, 2, COLS])
        probs2T = A2("probs2T", [P, 2, COLS])
        bias_c = A2("bias_c", [P, 4, 2 * P])
        A2h = Area(hT_at)
        cT_hi = A2h("cT_hi", [P, 4, 2 * P], F32R)
        cT_lo = A2h("cT_lo", [P, 4, 2 * P], F32R)
        A2q = Area(hT_at)
        qrT = A2q("qrT", [ROPE, HA, 2 * P])
        krT = A2h("krT", [ROPE, 2 * P])
        kaT = A2h("kaT", [P, HA, 2 * P])
        qaT = A2h("qaT", [P, HA, 2 * P])
        A2b = Area(A2h.end)
        bias_d = A2b("bias_d", [P, 4, 2 * P])
        rt = A2h("rt", [P, 2, COLS])
        lam4 = A2h("lam4", [P, 4, HD])
        lamt = A2h("lamt", [P, 2, HD])
        subln = A2h("subln", [P, P])
        dtmp = A2h("dtmp", [P, 2, P])
        A2m = Area(work_at)
        u_nat = A2m("u_nat", [P, 2, TOK, COLS])
        uT_hi = A2m("uT_hi", [P, UPC // P, 2 * P], F32R)
        uT_lo = A2m("uT_lo", [P, UPC // P, 2 * P], F32R)
        A3 = Area(work_at)
        frow = A3("frow", [P, D])
        fout = A3("fout", [P, TOK, D])
        for area, end in ((A1, nc.sbuf_usable_end), (A2, nc.sbuf_usable_end), (A2m, nc.sbuf_usable_end),
                          (A1k, hT_at + 4 * (QH + KVH) * 2 * P), (A1h, hT_at + 8 * KC * 2 * P), (A2h, hT_at + 8 * KC * 2 * P)):
            assert area.end <= end, (area.start, area.end, end)

        ps = ctx.enter_context(nc.psum_tensor("ps", [P, 8, COLS], F32))

        def sem(name):
            return ctx.enter_context(nc.semaphore(name))

        raw_landed = [sem(f"raw_landed{i}") for i in range(RAW_SLOTS)]
        class S:
            x_landed = sem("x_landed")
            const_landed = sem("const_landed")
            small_landed = sem("small_landed")
            rows_landed = sem("rows_landed")
            out_stored = sem("out_stored")
            hi_ready = sem("hi_ready")
            group_read = sem("group_read")
            group_multiplied = sem("group_multiplied")
            act_evacuated = sem("act_evacuated")
            dve_evacuated = sem("dve_evacuated")
            act_bank_filled = sem("act_bank_filled")
            act_bank_drained = sem("act_bank_drained")
            dve_bank_filled = sem("dve_bank_filled")
            dve_bank_drained = sem("dve_bank_drained")
            act_step = sem("act_step")
            dve_step = sem("dve_step")
            pool_step = sem("pool_step")
            pe_step = sem("pe_step")
            lhs_hi = sem("lhs_hi")
            lhs_ready = sem("lhs_ready")
            squares_ready = sem("squares_ready")
            var_ready = sem("var_ready")
            rstd_ready = sem("rstd_ready")
            rotated = sem("rotated")
            neg_max_ready = sem("neg_max_ready")
            probs_ready = sem("probs_ready")
            hcol_ready = sem("hcol_ready")
            gla_factor = sem("gla_factor")
            gla_q = sem("gla_q")
            gla_k = sem("gla_k")
            gla_logits = sem("gla_logits")
            gla_ln = sem("gla_ln")
            gla_dist = sem("gla_dist")
            xn_ready = sem("xn_ready")
            y_ready = sem("y_ready")
            x_ready = sem("x_ready")
            u_ready = sem("u_ready")
            uT_ready = sem("uT_ready")
            lam_in = sem("lam_in")
            lam_exp = sem("lam_exp")
            tables = sem("tables")
            final_ready = sem("final_ready")
            ang_ready = sem("ang_ready")

        jobs = {}
        order = []
        state = dict(G=0, L=0, T=0, act=0, dve=0)

        def plan(job):
            job.G, job.L, job.T = state["G"], state["L"], state["T"]
            job.E = state[job.evac]
            n = job.tiles * len(job.groups)
            state["G"] += n
            state["L"] += n
            state["T"] += job.tiles
            state[job.evac] += job.tiles
            jobs[job.name] = job
            order.append(job)

        MOD_TILES = 3 * D // COLS
        MOD_GROUPS = KC // 2
        mod_at = {}
        hT = (hT_hi, hT_lo)
        for l in range(DEPTH):
            mod_at[l] = state["G"]
            state["G"] += MOD_TILES * MOD_GROUPS
            w = io["w_in"][l]
            plan(Job(f"in{l}", w, KC, C_CG, COLS, hT))
            plan(Job(f"cg{l}", w, KC, RANK, RANK, hT, col0=C_CG))
            plan(Job(f"z{l}", w, KC, D, COLS, hT, col0=C_Z))
            plan(Job(f"out{l}", io["w_out"][l], KC, D, COLS, hT))
        for l in range(DEPTH):
            w = io["w_in_2"][l]
            plan(Job(f"c2{l}", w, KC, COLS, COLS, hT))
            plan(Job(f"kr{l}", w, KC, ROPE, ROPE, hT, col0=C_KR))
            plan(Job(f"in2{l}", w, KC, W2 - C_QB, COLS, hT, col0=C_QB))
            plan(Job(f"uq{l}", io["w_uq_2"][l], 3, HA * (NOPE + ROPE), COLS, (cT_hi, cT_lo)))
            plan(Job(f"ukv{l}", io["w_ukv_2"][l], 1, HA * (NOPE + VA), COLS, (cT_hi, cT_lo), lhs0=3))
            plan(Job(f"o2{l}", io["w_o_2"][l], KC, D, COLS, hT, evac="dve"))
            for h in range(2):
                plan(Job(f"up{l}{h}", io["w_up_2"][l], KC, UPC, COLS, hT, col0=h * UPC))
                plan(Job(f"down{l}{h}", io["w_down_2"][l, h * UPC:(h + 1) * UPC], UPC // P, D, COLS,
                         (uT_hi, uT_lo), evac="dve"))

        def groups(job, i):
            n = len(job.groups)
            for j, (k0, cnt) in enumerate(job.groups):
                yield j, job.G + i * n + j, job.L + i * n + j, k0, cnt

        def bank(job, i, t):
            return 2 * ((job.T + i) % 2) + t

        def tile_multiplied(job, i):
            return job.L + (i + 1) * len(job.groups)


        block = ctx.enter_context(nc.Block())

        class Mixer:

            def __init__(self, heads, dk, dv, scale, probs, probsT):
                self.heads, self.dk, self.dv, self.scale, self.probs, self.probsT = heads, dk, dv, scale, probs, probsT
                self.groups = ([(0, list(range(h, h + 4))) for h in range(0, heads, 4)]
                               + [(1, list(range(h, h + 2))) for h in range(0, heads, 2)])

        def repeat(ap, times):
            return ap.unsqueeze(1).broadcast_to([ap.shape[0], times, ap.shape[-1]])

        def spread(ap, times):
            return ap.unsqueeze(2).broadcast_to([ap.shape[0], ap.shape[-1], times])

        def head_pairs(src, col, stride, width, heads, dst):
            return [(dst[0:width, h:h + 2].rearrange("p h n -> p (h n)"),
                     [src[:, t, col + (h + a) * stride:col + (h + a) * stride + width]
                      for a in range(2) for t in range(TOK)], width) for h in range(0, heads, 2)]

        swa = Mixer(QH, HD, HD, HD ** -0.5, probs, probsT)
        swa.qk = lambda h: [(q1T[:, h], k1T[:, h // (QH // KVH)])]
        swa.v = lambda h, kk: proj[:, kk, C_V + (h // 4) * HD:C_V + (h // 4 + 1) * HD]
        swa.prep = head_pairs(proj, C_Q, HD, HD, QH, q1T) + head_pairs(proj, C_K, HD, HD, KVH, k1T)
        swa.masks = lambda t, hs: [(0, len(hs), repeat(K["swa"][:, (1 - t) * P:], len(hs)))]
        swa.out = lambda t, h, n: proj[:, t, C_Q + h * HD:C_Q + (h + n) * HD]

        mla = Mixer(HA, P, VA, (NOPE + ROPE) ** -0.5, probs2, probs2T)
        mla.qk = lambda h: [(qaT[:, h], kaT[:, h]), (qrT[:, h], krT[:])]
        mla.v = lambda h, kk: kv[:, kk, h * 256 + NOPE:(h + 1) * 256]
        mla.prep = (head_pairs(qm, 0, 192, NOPE, HA, qaT) + head_pairs(qm, NOPE, 192, ROPE, HA, qrT)
                    + head_pairs(kv, 0, 256, NOPE, HA, kaT)
                    + [(krT[:], [proj2[:, t, C_KR:C_KR + ROPE] for t in range(TOK)], ROPE)])
        mla.masks = lambda t, hs: [(0, len(hs), repeat(K["chunk"][:, (1 - t) * P:], len(hs)))]
        mla.out = lambda t, h, n: y2[:, t, h * VA:(h + n) * VA]

        dif = Mixer(8, HD, P, HD ** -0.5, probs2, probs2T)
        dif.qk = lambda u: [(qaT[0:HD, u], kaT[0:HD, u])]
        dif.v = lambda u, kk: proj2[:, kk, C_VB + (u // 2) * P:C_VB + (u // 2 + 1) * P]
        dif.prep = head_pairs(proj2, C_QB, HD, HD, 8, qaT) + head_pairs(proj2, C_KB, HD, HD, 8, kaT)
        dif.masks = lambda t, hs: [(j, j + 2, repeat(bias_d[:, hs[j] // 2, (1 - t) * P:], 2)) for j in range(0, len(hs), 2)]
        dif.out = lambda t, u, n: y2[:, t, HA * VA + (u // 2) * P:HA * VA + (u // 2 + 1) * P]

        chk = Mixer(4, P, P, P ** -0.5, probs2, probs2T)
        chk.qk = lambda h: [(qaT[:, h], kaT[:, h])]
        chk.v = lambda h, kk: proj2[:, kk, C_VC + h * P:C_VC + (h + 1) * P]
        chk.prep = head_pairs(proj2, C_QC, P, P, 4, qaT) + head_pairs(proj2, C_KC, P, P, 4, kaT)
        chk.masks = lambda t, hs: [(0, len(hs), bias_c[:, hs[0]:hs[0] + len(hs), (1 - t) * P:])]
        chk.out = lambda t, h, n: y2[:, t, HA * VA + 4 * P + h * P:HA * VA + 4 * P + (h + n) * P]

        ROWS1 = 5
        ROWS2 = 4

        def rows_value(block, l, part=None):
            if block == 1:
                return 16 * (ROWS1 * l + (2 if part == "mod" else ROWS1))
            return 16 * (ROWS1 * DEPTH + ROWS2 * (l + 1))

        def rstd_value(l, k):
            return 4 * DEPTH + 4 * l + k + 1

        def x_complete(eng, l, half):
            if half == 1:
                eng.wait_ge(S.dve_evacuated, jobs[f"o2{l}"].E + 4)
            elif l:
                eng.wait_ge(S.dve_evacuated, jobs[f"down{l - 1}1"].E + 4)
            else:
                eng.wait_ge(S.x_ready, DEPTH)

        @block.sync
        def _(sp):
            def load(G, src, cnt, width):
                slot = G % RAW_SLOTS
                if G >= RAW_SLOTS:
                    sp.wait_ge(S.group_read, G - RAW_SLOTS + 1)
                dst = raw[:, slot, 0:cnt * width].rearrange("p (c n) -> p c n", c=cnt)
                sp.dma_start(dst, src.rearrange("(c p) n -> p c n", p=P)).then_inc(raw_landed[slot], 16)

            def weights(job):
                for i in range(job.tiles):
                    c0 = job.col0 + i * job.width
                    for j, G, L, k0, cnt in groups(job, i):
                        load(G, job.w[k0 * P:(k0 + cnt) * P, c0:c0 + job.width], cnt, job.width)

            sp.dma_start(c_col[:], io["c"]).then_inc(S.const_landed, 16)
            sp.dma_start(cst[:], io["const"]).then_inc(S.const_landed, 16)
            sp.dma_start(cols1[:], io["cols1"]).then_inc(S.const_landed, 16)
            sp.dma_start(x[:], io["x"][0].rearrange("(t p) n -> p t n", p=P)).then_inc(S.x_landed, 16)
            for l in range(DEPTH):
                for t in range(MOD_TILES):
                    for g in range(MOD_GROUPS):
                        load(mod_at[l] + t * MOD_GROUPS + g,
                             io["w_mod"][l, 2 * g * P:2 * (g + 1) * P, t * COLS:(t + 1) * COLS], 2, COLS)
                for name in ("in", "cg", "z", "out"):
                    weights(jobs[f"{name}{l}"])
            for l in range(DEPTH):
                for name in ("c2", "kr", "in2", "uq", "ukv", "o2"):
                    weights(jobs[f"{name}{l}"])
                for h in range(2):
                    weights(jobs[f"up{l}{h}"])
                    weights(jobs[f"down{l}{h}"])
            for t in range(TOK):
                sp.wait_ge(S.final_ready, t + 1)
                sp.dma_start(io["out"][0, t * P:(t + 1) * P], fout[:, t]).then_inc(S.out_stored, 16)
            sp.wait_ge(S.out_stored, 16 * TOK)

        @block.gpsimd
        def _(pool):
            n = Tally()

            def rsqrt(cnt):
                pool.wait_ge(S.var_ready, n(S.var_ready))
                pool.tensor_tensor(stat[:, 8:8 + cnt], stat[:, 0:cnt], minus_half[:, 0:cnt], ALU.pow
                                   ).then_inc(S.rstd_ready, 1)

            pool.memset(minus_half[:], -0.5).then_inc(S.pool_step, 1)
            pool.wait_ge(S.pool_step, 1)
            for dst, src in ((cols2[:], io["cols2"]), (stat[:, 32:34].bitcast(I32), io["positions"]),
                             (sinks[:], io["swa_sinks"].partition_broadcast(P)),
                             (gnorm[:], io["gla_norm_g"].partition_broadcast(P)),
                             (gup[:], io["gla_w_gate_up"].rearrange("l r n -> r l n")),
                             (levels[:], io["levels"].rearrange("p (l n) -> p l n", n=P))):
                pool.dma_start(dst, src).then_inc(S.small_landed, 16)
            for l in range(DEPTH):
                if l:
                    pool.wait_ge(S.x_ready, l)
                pool.dma_start(modrow[:, 0, 0:D], io["b_mod"][l, 2 * D:].partition_broadcast(P)
                               ).then_inc(S.rows_landed, 16)
                pool.dma_start(modrow[:, 1, 0:D], io["g_post"][l].partition_broadcast(P)
                               ).then_inc(S.rows_landed, 16)
                rsqrt(2)
                pool.wait_ge(S.group_multiplied, tile_multiplied(jobs[f"z{l}"], 3))
                pool.dma_start(sgw[:], io["sg_w"][l].rearrange("g t s -> t g s")).then_inc(S.rows_landed, 16)
                pool.dma_start(sgln[:, 0], io["sg_ln_g"][l].partition_broadcast(P)).then_inc(S.rows_landed, 16)
                pool.dma_start(sgln[:, 1], io["sg_ln_b"][l].partition_broadcast(P)).then_inc(S.rows_landed, 16)
                rsqrt(2)
                for lev in range(1, LEVELS + 2):
                    pool.wait_ge(S.gla_q, n(S.gla_q))
                    pool.tensor_tensor(klev[:, lev % 2], glf[:, lev % 2], gq[:, 1], ALU.mult).then_inc(S.gla_k, 1)
                rsqrt(8)
                rsqrt(2)
            for l in range(DEPTH):
                x_complete(pool, l, 0)
                r = io["rel"]
                pool.dma_start(bias_c[:], bass.AP(tensor=r.tensor, offset=l * 4 * REL_PAD + 1,
                                                  ap=[[1, P], [REL_PAD, 4], [1, 2 * P]])).then_inc(S.rows_landed, 16)
                rsqrt(2)
                rsqrt(4)
                pool.dma_start(lam4[:], io["lambdas"][l].partition_broadcast(P)).then_inc(S.rows_landed, 16)
                pool.dma_start(subln[:], io["diff_subln_2"][l].partition_broadcast(P)).then_inc(S.rows_landed, 16)
                pool.wait_ge(S.rotated, DEPTH + l + 1)
                pool.dma_start(bias_d[:], io["diff_bias"].rearrange("p (h k) -> p h k", h=4)).then_inc(S.rows_landed, 16)
                rsqrt(8)
                rsqrt(2)
            pool.wait_ge(S.dve_evacuated, jobs["down11"].E + 4)
            pool.dma_start(frow[:], io["final_norm_2"].partition_broadcast(P)).then_inc(S.rows_landed, 16)
            rsqrt(2)

        @block.scalar
        def _(act):
            n = Tally()

            def link(ins):
                ins.then_inc(S.act_step, 1)
                act.wait_ge(S.act_step, n(S.act_step))

            def hi(job, i, js):
                for j, G, L, k0, cnt in list(groups(job, i))[js]:
                    act.wait_ge(raw_landed[G % RAW_SLOTS], 16 * (G // RAW_SLOTS + 1))
                    if L >= SPLIT_SLOTS:
                        act.wait_ge(S.group_multiplied, L - SPLIT_SLOTS + 1)
                    w = cnt * job.width
                    act.activation(w_hi[:, L % SPLIT_SLOTS, 0:w], raw[:, G % RAW_SLOTS, 0:w], ACT.Copy
                                   ).then_inc(S.hi_ready, 1)

            def evacuate(job, i):
                act.wait_ge(S.group_multiplied, tile_multiplied(job, i))
                kind, l = job.name[:-1], int(job.name[-1])
                if kind in ("up0", "up1"):
                    h, l = int(job.name[-1]), int(job.name[-2])
                if kind == "up0" or kind == "up1":
                    done = 2 * job.tiles * (2 * l + h)
                    if i >= 2 or done:
                        act.wait_ge(S.uT_ready, done + 2 * max(i - 1, 0))
                    for t in range(TOK):
                        a = act.activation(u_nat[:, i % 2, t], ps[:, bank(job, i, t)], ACT.Relu, scale=stat[:, 8 + t:9 + t])
                        a.then_inc(S.act_evacuated if t else S.act_step, 1)
                    act.wait_ge(S.act_step, n(S.act_step))
                    act.wait_ge(S.act_evacuated, job.E + i + 1)
                    u = u_nat[:, i % 2].rearrange("p t n -> p (t n)")
                    act.activation(u, u, ACT.Square).then_inc(S.u_ready, 1)
                    return
                for t in range(TOK):
                    src = ps[:, bank(job, i, t), 0:job.width]
                    c = job.col0 + i * job.width
                    f, scale = ACT.Copy, 1.0
                    if kind in ("in", "cg"):
                        dst = proj[:, t, c:c + job.width]
                        f = ACT.Gelu_apprx_tanh if C_SU <= c < C_CQ else ACT.Copy
                    elif kind == "z":
                        dst, f = proj[:, t, c:c + job.width], ACT.Silu
                    elif kind == "out":
                        dst = out_sb[:, t, c:c + job.width]
                        link(act.activation(probs[:, t], src, ACT.Square, accum_out=stat[:, 16 + 4 * t + i:17 + 4 * t + i]))
                    elif kind in ("c2", "kr", "in2"):
                        dst, scale = proj2[:, t, c:c + job.width], stat[:, 8 + t:9 + t]
                    elif kind == "uq":
                        dst, scale = qm[:, t, c:c + job.width], stat[:, 8 + t:9 + t]
                    else:
                        dst, scale = kv[:, t, c:c + job.width], stat[:, 10 + t:11 + t]
                    a = act.activation(dst, src, f, scale=scale)
                    a.then_inc(S.act_evacuated if t else S.act_step, 1)
                n(S.act_step)

            def stream(job, prev, start=0):
                for i in range(start, job.tiles):
                    hi(job, i, slice(0, 2))
                    if prev:
                        evacuate(*prev)
                    hi(job, i, slice(2, None))
                    prev = (job, i) if job.evac == "act" else None
                return prev

            def split_bank(dst, b, scale=None, bias=None):
                act.wait_ge(S.act_bank_filled, n(S.act_bank_filled))
                u = n(S.lhs_hi) - 1
                if u >= 2:
                    act.wait_ge(S.lhs_ready, u - 1)
                src = ps[:, 6 + (n.so_far(S.act_bank_filled) - 1) % 2]
                if scale is None:
                    act.activation(hf[:, u % 2].rearrange("p c n -> p (c n)"), src, ACT.Copy).then_inc(S.act_bank_drained, 1)
                    act.wait_ge(S.act_bank_drained, n.so_far(S.act_bank_filled))
                else:
                    for c in range(2):
                        k = 2 * b + c
                        kw = {"bias": bias[:, k:k + 1]} if bias is not None else {}
                        a = act.activation(hf[:, u % 2, c], src[:, c * 2 * P:(c + 1) * 2 * P],
                                           ACT.Identity if kw else ACT.Copy, scale=scale[:, k:k + 1], **kw)
                        a.then_inc(S.act_bank_drained if c else S.act_step, 1)
                    act.wait_ge(S.act_step, n(S.act_step))
                    act.wait_ge(S.act_bank_drained, n.so_far(S.act_bank_filled))
                act.activation(dst[:, 2 * b:2 * b + 2].rearrange("p c n -> p (c n)"),
                               hf[:, u % 2].rearrange("p c n -> p (c n)"), ACT.Copy).then_inc(S.lhs_hi, 1)

            def first_tile(job, banks, dst, scale=None, bias=None):
                split_bank(dst, 0, scale, bias)
                for j in range(max(banks, len(job.groups))):
                    if j + 1 < banks:
                        split_bank(dst, j + 1, scale, bias)
                    if j < len(job.groups):
                        hi(job, 0, slice(j, j + 1))
                return (job, 0) if job.evac == "act" else None

            def squares(srcs, junk):
                for j, s in enumerate(srcs):
                    w = s.shape[-1]
                    a = act.activation(junk[:, 0:w], s, ACT.Square, accum_out=stat[:, j:j + 1])
                    a.then_inc(S.squares_ready, 1)
                    act.wait_ge(S.squares_ready, n(S.squares_ready))

            def bank_copy(dst, width=COLS, scale=1.0):
                act.wait_ge(S.act_bank_filled, n(S.act_bank_filled))
                b = 6 + (n.so_far(S.act_bank_filled) - 1) % 2
                act.activation(dst, ps[0:dst.shape[0], b, 0:width], ACT.Copy, scale=scale).then_inc(S.act_bank_drained, 1)

            def attention(m):
                for dst, sources, rows in m.prep:
                    bank_copy(dst, len(sources) * P)

                def exps(g):
                    t, hs = m.groups[g]
                    nk = (t + 1) * P
                    act.wait_ge(S.neg_max_ready, n(S.neg_max_ready))
                    for j in range(len(hs)):
                        e = m.probs[:, g % 2, j * nk:(j + 1) * nk]
                        a = act.activation(e, e, ACT.Exp, bias=smax[:, g % 2, j:j + 1], accum_out=ssum[:, g % 2, j:j + 1])
                        if m is swa or j < len(hs) - 1:
                            link(a)
                    if m is swa:
                        a = act.activation(ses[:, g % 2, 0:len(hs)], ses[:, g % 2, 0:len(hs)], ACT.Exp)
                    a.then_inc(S.probs_ready, 1)
                exps(0)
                for g in range(len(m.groups)):
                    if g + 1 < len(m.groups):
                        exps(g + 1)
                    bank_copy(m.probsT[:, g % 2])

            act.wait_ge(S.const_landed, 48)
            link(act.activation(c_col[:], c_col[:], ACT.Silu))
            act.wait_ge(S.tables, 1)
            act.activation(cs1[:].rearrange("p a t n -> p (a t n)"), cs1[:].rearrange("p a t n -> p (a t n)"), ACT.Sin
                           ).then_inc(S.ang_ready, 1)
            act.wait_ge(S.x_landed, 16)
            for l in range(DEPTH):
                if l:
                    act.wait_ge(S.x_ready, l)
                squares([x[:, 0], x[:, 1]], proj[:, 0, D:2 * D])
                act.wait_ge(S.hcol_ready, l + 1)
                job = jobs[f"in{l}"]
                prev = first_tile(job, KC // 2, hT_hi, hcol[:, 0], hcol[:, 1])
                prev = stream(job, prev, 1)
                prev = stream(jobs[f"cg{l}"], prev)
                prev = stream(jobs[f"z{l}"], prev)
                evacuate(*prev)
                attention(swa)
                bank_copy(cgT[:], 2 * P)
                bank_copy(gq[:, 0].rearrange("p k n -> p (k n)"), scale=GDK ** -0.5)
                bank_copy(gq[:, 1].rearrange("p k n -> p (k n)"))
                act.wait_ge(S.gla_logits, l + 1)
                f = lambda ap: ap.rearrange("p k n -> p (k n)")
                link(act.activation(f(gle[:, 0]), f(gle[:, 0]), ACT.Exp, scale=-1.0))
                act.activation(f(gle[:, 0]), f(gle[:, 0]), ACT.Ln, bias=K["ones"][:, 0:1]).then_inc(S.gla_ln, 1)
                for lev in range(1, LEVELS + 2):
                    act.wait_ge(S.gla_dist, n(S.gla_dist))
                    if lev >= 3:
                        act.wait_ge(S.gla_k, l * (LEVELS + 1) + lev - 2)
                    link(act.activation(f(gle[:, lev % 2]), f(gle[:, lev % 2]), ACT.Abs))
                    act.activation(f(glf[:, lev % 2]), f(gle[:, lev % 2]), ACT.Exp, scale=-1.0 / 16).then_inc(S.gla_factor, 1)
                job = jobs[f"out{l}"]
                prev = stream(job, first_tile(job, KC // 2, hT_hi), 1)
                evacuate(*prev)
            for l in range(DEPTH):
                x_complete(act, l, 0)
                if l == 0:
                    act.wait_ge(S.small_landed, 16 * 6)
                squares([x[:, 0], x[:, 1]], y2[:, 0])
                act.wait_ge(S.rstd_ready, rstd_value(l, 0))
                job = jobs[f"c2{l}"]
                prev = first_tile(job, KC // 2, hT_hi, cols2[:, l, 0:KC])
                for name in ("kr", "in2"):
                    prev = stream(jobs[f"{name}{l}"], prev)
                evacuate(*prev)
                squares([proj2[:, t, a:b] for a, b in ((C_CQ2, C_CKV), (C_CKV, C_KR)) for t in range(TOK)], y2[:, 0])
                act.wait_ge(S.rstd_ready, rstd_value(l, 1))
                job = jobs[f"uq{l}"]
                prev = stream(job, first_tile(job, 2, cT_hi, cols2[:, l, 32:36]), 1)
                prev = stream(jobs[f"ukv{l}"], prev)
                evacuate(*prev)
                attention(mla)
                act.wait_ge(S.lam_in, l + 1)
                act.activation(stat[:, 48:50], stat[:, 48:50], ACT.Exp).then_inc(S.lam_exp, 1)
                attention(dif)
                attention(chk)
                job = jobs[f"o2{l}"]
                stream(job, first_tile(job, KC // 2, hT_hi), 1)
                x_complete(act, l, 1)
                squares([x[:, 0], x[:, 1]], y2[:, 0])
                act.wait_ge(S.rstd_ready, rstd_value(l, 3))
                job = jobs[f"up{l}0"]
                prev = stream(job, first_tile(job, KC // 2, hT_hi, cols2[:, l, KC:2 * KC]), 1)
                prev = stream(jobs[f"down{l}0"], prev)
                prev = stream(jobs[f"up{l}1"], prev)
                prev = stream(jobs[f"down{l}1"], prev)
            act.wait_ge(S.dve_evacuated, jobs["down11"].E + 4)
            squares([x[:, 0], x[:, 1]], fout[:, 0])

        @block.vector
        def _(dve):
            n = Tally()

            def link(ins):
                ins.then_inc(S.dve_step, 1)
                dve.wait_ge(S.dve_step, n(S.dve_step))

            def lo(job, i, js):
                for j, G, L, k0, cnt in list(groups(job, i))[js]:
                    dve.wait_ge(S.hi_ready, L + 1)
                    w, s = cnt * job.width, L % SPLIT_SLOTS
                    dve.tensor_tensor(w_lo[:, s, 0:w], raw[:, G % RAW_SLOTS, 0:w], w_hi[:, s, 0:w].bitcast(F32), ALU.subtract
                                      ).then_inc(S.group_read, 1)

            def evacuate(job, i):
                dve.wait_ge(S.group_multiplied, tile_multiplied(job, i))
                if job.E + i:
                    dve.wait_ge(S.dve_evacuated, job.E + i)
                for t in range(TOK):
                    v = x[:, t, i * COLS:(i + 1) * COLS]
                    a = dve.tensor_tensor(v, v, ps[:, bank(job, i, t)], ALU.add)
                    if t == 0:
                        link(a)
                a.then_inc(S.dve_evacuated, 1)

            def stream(job, prev=None, start=0):
                for i in range(start, job.tiles):
                    lo(job, i, slice(0, 2))
                    if prev:
                        evacuate(*prev)
                    lo(job, i, slice(2, None))
                    prev = (job, i) if job.evac == "dve" else None
                return prev

            def split_bank(dst_hi, dst_lo, b):
                dve.wait_ge(S.lhs_hi, n(S.lhs_hi))
                u = n.so_far(S.lhs_hi) - 1
                f = lambda ap: ap.rearrange("p c n -> p (c n)")
                dve.tensor_tensor(f(dst_lo[:, 2 * b:2 * b + 2]), f(hf[:, u % 2]),
                                  f(dst_hi[:, 2 * b:2 * b + 2]).bitcast(F32), ALU.subtract).then_inc(S.lhs_ready, 1)

            def first_tile(job, banks, dst_hi, dst_lo):
                split_bank(dst_hi, dst_lo, 0)
                for j in range(max(banks, len(job.groups))):
                    if j + 1 < banks:
                        split_bank(dst_hi, dst_lo, j + 1)
                    if j < len(job.groups):
                        lo(job, 0, slice(j, j + 1))
                return (job, 0) if job.evac == "dve" else None

            def dve_bank():
                u = n(S.dve_bank_filled)
                dve.wait_ge(S.dve_bank_filled, u)
                return 4 + (u - 1) % 2

            def drained(ins):
                ins.then_inc(S.dve_bank_drained, 1)
                dve.wait_ge(S.dve_bank_drained, n(S.dve_bank_drained))

            def mean_squares(parts, cnt):
                dve.wait_ge(S.squares_ready, n(S.squares_ready, cnt))
                variance(parts)

            def variance(parts):
                for j, (a, b, width) in enumerate(parts):
                    v = dve.tensor_scalar(stat[:, a:b], stat[:, a:b], 1.0 / width, EPS, ALU.mult, ALU.add)
                    if j < len(parts) - 1:
                        link(v)
                v.then_inc(S.var_ready, 1)
                n(S.var_ready)

            def rstd():
                dve.wait_ge(S.rstd_ready, n.so_far(S.var_ready))

            def rotate(heads_at, cos, sin, half, tmp):
                t1, t2 = heads_at(0, half), heads_at(half, 2 * half)
                a, b, c, d = tmp
                link(dve.tensor_tensor(a, t1, cos, ALU.mult))
                link(dve.tensor_tensor(b, t2, sin, ALU.mult))
                link(dve.tensor_tensor(c, t2, cos, ALU.mult))
                link(dve.tensor_tensor(d, t1, sin, ALU.mult))
                link(dve.tensor_tensor(t1, a, b, ALU.subtract))
                return dve.tensor_tensor(t2, c, d, ALU.add)

            def attention(m, l):
                def softmax(g):
                    t, hs = m.groups[g]
                    nk, nh = (t + 1) * P, len(hs)
                    b = dve_bank()
                    s = ps[:, b].rearrange("p (h k) -> p h k", h=nh)
                    e = m.probs[:, g % 2].rearrange("p (h k) -> p h k", h=nh)
                    masks = m.masks(t, hs)
                    for j0, j1, mask in masks:
                        a = dve.scalar_tensor_tensor(out=e[:, j0:j1], in0=s[:, j0:j1], scalar=m.scale, in1=mask,
                                                     op0=ALU.mult, op1=ALU.add)
                        if j1 < nh:
                            link(a)
                    drained(a)
                    a = dve.tensor_reduce(smax[:, g % 2, 0:nh], e, AX.X, ALU.max, negate=True)
                    if m is swa:
                        link(a)
                        k = slice(hs[0], hs[0] + nh)
                        link(dve.tensor_tensor(smax[:, g % 2, 0:nh], smax[:, g % 2, 0:nh], neg_sinks[:, l, k], ALU.min))
                        a = dve.tensor_tensor(ses[:, g % 2, 0:nh], smax[:, g % 2, 0:nh], sinks[:, l, k], ALU.add)
                    a.then_inc(S.neg_max_ready, 1)

                def out(g):
                    t, hs = m.groups[g]
                    nh = len(hs)
                    b = dve_bank()
                    den, rec = ssum[:, g % 2, 0:nh], srec[:, g % 2, 0:nh]
                    if m is swa:
                        den = sden[:, g % 2, 0:nh]
                        link(dve.tensor_tensor(den, ssum[:, g % 2, 0:nh], ses[:, g % 2, 0:nh], ALU.add))
                    link(dve.reciprocal(rec, den))
                    o = ps[:, b, 0:nh * m.dv].rearrange("p (h d) -> p h d", h=nh)
                    if m is not dif:
                        drained(dve.tensor_tensor(m.out(t, hs[0], nh).rearrange("p (h d) -> p h d", h=nh), o,
                                                  spread(rec, m.dv), ALU.mult))
                        return
                    link(dve.tensor_scalar(sden[:, g % 2, 0:nh], rec, stat[:, 52:53], None, ALU.mult))
                    for j in range(0, nh, 2):
                        link(dve.tensor_scalar(dtmp[:, 0], o[:, j + 1], sden[:, g % 2, j + 1:j + 2], None, ALU.mult))
                        a = dve.scalar_tensor_tensor(out=m.out(t, hs[j], 1), in0=o[:, j], scalar=rec[:, j:j + 1],
                                                     in1=dtmp[:, 0], op0=ALU.mult, op1=ALU.subtract)
                        if j + 2 < nh:
                            link(a)
                    drained(a)
                softmax(0)
                for g in range(len(m.groups)):
                    if g + 1 < len(m.groups):
                        softmax(g + 1)
                    out(g)

            dve.wait_ge(S.const_landed, 48)
            dve.wait_ge(S.small_landed, 16 * 6)
            link(dve.tensor_copy(stat[:, 34:36], stat[:, 32:34].bitcast(I32)))
            for t in range(TOK):
                link(dve.tensor_scalar(cs1[:, 1, t], K["inv_freq"], stat[:, 34 + t:35 + t], None, ALU.mult))
            ang, turn = cs1[:, 1].rearrange("p t n -> p (t n)"), turns[:]
            for part, quarter in ((0, 0.25), (1, 0.0)):
                r = cs1[:, part].rearrange("p t n -> p (t n)")
                link(dve.tensor_scalar(turn, ang, 1.0 / (2 * np.pi), quarter, ALU.mult, ALU.add))
                link(dve.tensor_scalar(turn, turn, ROUND, None, ALU.add))
                link(dve.tensor_scalar(turn, turn, ROUND, None, ALU.subtract))
                for j, c in enumerate(TWO_PI):
                    link(dve.scalar_tensor_tensor(out=r, in0=turn, scalar=-c, in1=ang if j == 0 else r,
                                                  op0=ALU.mult, op1=ALU.add))
                link(dve.tensor_scalar(r, r, float(np.pi / 2) if part == 0 else 0.0, None, ALU.add))
                a = dve.tensor_scalar(r, r, PI_BELOW, -PI_BELOW, ALU.min, ALU.max)
                if part == 0:
                    link(a)
            a.then_inc(S.tables, 1)
            link(dve.tensor_scalar(neg_sinks[:], sinks[:], -1.0, None, ALU.mult))
            dve.wait_ge(S.ang_ready, 1)

            for l in range(DEPTH):
                def mod_out(t):
                    b = dve_bank()
                    if t < 4:
                        drained(dve.tensor_tensor(hcol[:, 1, 4 * t:4 * t + 4], ps[:, b, 0:4],
                                                  cols1[:, l, 16 + 4 * t:20 + 4 * t], ALU.add))
                    elif t < 8:
                        k = 4 * (t - 4)
                        drained(dve.tensor_tensor(stat[:, 40:44], ps[:, b, 0:4], cols1[:, l, 16 + 4 * t:20 + 4 * t], ALU.add))
                        a = dve.scalar_tensor_tensor(out=hcol[:, 0, k:k + 4], in0=stat[:, 40:44], scalar=1.0,
                                                     in1=cols1[:, l, k:k + 4], op0=ALU.add, op1=ALU.mult)
                        if t < 7:
                            link(a)
                        else:
                            a.then_inc(S.hcol_ready, 1)
                    else:
                        k = slice((t - 8) * COLS, (t - 7) * COLS)
                        dve.wait_ge(S.rows_landed, rows_value(1, l, "mod"))
                        drained(dve.tensor_tensor(gp[:, k], ps[:, b], modrow[:, 0, k], ALU.add))
                        link(dve.tensor_tensor(gp[:, k], gp[:, k], modrow[:, 1, k], ALU.mult))

                mean_squares([(0, 2, D)], 2)
                for t in range(MOD_TILES):
                    for g in range(MOD_GROUPS):
                        G = mod_at[l] + t * MOD_GROUPS + g
                        dve.wait_ge(raw_landed[G % RAW_SLOTS], 16 * (G // RAW_SLOTS + 1))
                        if G:
                            dve.wait_ge(S.group_read, G)
                        for a in range(2):
                            w = raw[:, G % RAW_SLOTS, a * COLS:(a + 1) * COLS]
                            c = c_col[:, 2 * g + a:2 * g + a + 1]
                            s = acc[:, t % 2, a]
                            if g == 0:
                                m = dve.tensor_scalar(s, w, c, None, ALU.mult)
                            else:
                                m = dve.scalar_tensor_tensor(out=s, in0=w, scalar=c, in1=s, op0=ALU.mult, op1=ALU.add)
                        m.then_inc(S.group_read, 1)
                    if t:
                        mod_out(t - 1)
                mod_out(MOD_TILES - 1)
                rstd()
                for t in range(TOK):
                    a = dve.tensor_scalar(xn[:, t, 0:D], x[:, t], stat[:, 8 + t:9 + t], None, ALU.mult)
                a.then_inc(S.xn_ready, 1)
                job = jobs[f"in{l}"]
                stream(job, first_tile(job, KC // 2, hT_hi, hT_lo), 1)
                stream(jobs[f"cg{l}"])
                stream(jobs[f"z{l}"])
                dve.wait_ge(S.act_evacuated, jobs[f"z{l}"].E + 4)
                heads = QH + KVH
                tmp = [acc[:, i // 2, i % 2, 0:heads * HALF].rearrange("p (h n) -> p h n", h=heads) for i in range(4)]
                for t in range(TOK):
                    qk = proj[:, t, 0:heads * HD].rearrange("p (h d) -> p h d", d=HD)
                    cos, sin = repeat(cs1[:, 0, t], heads), repeat(cs1[:, 1, t], heads)
                    r = rotate(lambda a, b: qk[:, :, a:b], cos, sin, HALF, tmp)
                    if t == 0:
                        link(r)
                r.then_inc(S.rotated, 1)
                v = proj[:, :, C_SV:C_SV + COLS]
                for t in range(TOK):
                    link(dve.bn_stats(bn[:, t], v[:, t]))
                    link(dve.bn_aggr(stat[:, 24 + 2 * t:26 + 2 * t], bn[:, t]))
                    a = dve.tensor_scalar(stat[:, t:t + 1], stat[:, 25 + 2 * t:26 + 2 * t], EPS, None, ALU.add)
                    if t == 0:
                        link(a)
                a.then_inc(S.var_ready, 1)
                n(S.var_ready)
                rstd()
                dve.wait_ge(S.rows_landed, rows_value(1, l))
                for t in range(TOK):
                    link(dve.tensor_scalar(v[:, t], v[:, t], stat[:, 24 + 2 * t:25 + 2 * t], stat[:, 8 + t:9 + t],
                                           ALU.subtract, ALU.mult))
                    link(dve.tensor_tensor(v[:, t], v[:, t], sgln[:, 0], ALU.mult))
                    link(dve.tensor_tensor(v[:, t], v[:, t], sgln[:, 1], ALU.add))
                attention(swa, l)
                for half in range(2):
                    b = dve_bank()
                    drained(dve.tensor_tensor(sgwT[:, 4 * half:4 * half + 4], ps[:, b].rearrange("p (g t) -> p g t", g=4),
                                              repeat(K["tril"], 4), ALU.mult))
                for half in range(2):
                    b = dve_bank()
                    for j in range(4):
                        g = 4 * half + j
                        u = proj[:, :, C_SU + g * SGD:C_SU + (g + 1) * SGD]
                        a = dve.scalar_tensor_tensor(out=u, in0=ps[:, b, j * P:(j + 1) * P].rearrange("p (n c) -> p n c", n=TOK),
                                                     scalar=cols1[:, l, 64 + g:65 + g], in1=u, op0=ALU.add, op1=ALU.mult)
                        if j < 3:
                            link(a)
                    drained(a)
                b = dve_bank()
                link(dve.tensor_scalar(glx[:, 0], ps[:, b, 0:2 * P], cols1[:, l, 72:73], None, ALU.add))
                drained(dve.tensor_scalar(glx[:, 1], ps[:, b, 2 * P:4 * P], cols1[:, l, 73:74], None, ALU.add))
                dve.scalar_tensor_tensor(out=gle[:, 0], in0=glx[:], scalar=-1.0, in1=glx[:], op0=ALU.mult, op1=ALU.max
                                         ).then_inc(S.gla_logits, 1)
                link(dve.memset(pairs[:, 0:2], 0.0))
                dve.wait_ge(S.gla_ln, l + 1)
                link(dve.scalar_tensor_tensor(out=glx[:], in0=glx[:], scalar=0.0, in1=gle[:, 0], op0=ALU.min, op1=ALU.subtract))
                for kt in range(2):
                    for t in range(TOK):
                        s = slice(t * P, (t + 1) * P)
                        link(dve.tensor_tensor_scan(glb[:, kt, s], K["ones"], glx[:, kt, s], 0.0, ALU.mult, ALU.add))

                def dist(lev):
                    e = gle[:, lev % 2]
                    if lev <= LEVELS:
                        n_b = 2 ** lev
                        g = glb[:].rearrange("p k (b n) -> p (k b) n", n=n_b)
                        mid = g[:, :, n_b // 2 - 1:n_b // 2].broadcast_to([P, 4 * P // n_b, n_b])
                        dve.tensor_tensor(e.rearrange("p k (b n) -> p (k b) n", n=n_b), g, mid, ALU.subtract
                                          ).then_inc(S.gla_dist, 1)
                    else:
                        link(dve.tensor_tensor(e[:, :, 0:P], glb[:, :, 0:P],
                                               glb[:, :, P - 1:P].broadcast_to([P, 2, P]), ALU.subtract))
                        dve.tensor_copy(e[:, :, P:2 * P], glb[:, :, P:2 * P]).then_inc(S.gla_dist, 1)

                def consume(lev):
                    for t in range(TOK if lev <= LEVELS else 1):
                        b = dve_bank()
                        if lev <= LEVELS:
                            drained(dve.copy_predicated(pairs[:, t].rearrange("p (h n) -> p h n", h=GH),
                                                        repeat(levels[:, lev], GH),
                                                        ps[:, b].rearrange("p (h n) -> p h n", h=GH)))
                        else:
                            drained(dve.tensor_copy(pairs[:, 2], ps[:, b]))
                dist(1)
                dist(2)
                for lev in range(1, LEVELS + 2):
                    dve.wait_ge(S.gla_factor, n(S.gla_factor))
                    dve.tensor_tensor(qlev[:, lev % 2], glf[:, lev % 2], gq[:, 0], ALU.mult).then_inc(S.gla_q, 1)
                    if lev + 2 <= LEVELS + 1:
                        dist(lev + 2)
                    consume(lev - 1)
                consume(LEVELS + 1)
                for t in range(TOK):
                    b = dve_bank()
                    drained(dve.tensor_copy(oc[:, t * COLS:(t + 1) * COLS], ps[:, b]))
                link(dve.tensor_tensor(osq, oc, oc, ALU.mult))
                link(dve.tensor_reduce(stat[:, 0:8], osq.rearrange("p (h d) -> p h d", h=8), AX.X, ALU.add))
                variance([(0, 8, GDV)])
                rstd()
                for t in range(TOK):
                    y = proj[:, t, C_CV:C_CV + COLS].rearrange("p (h d) -> p h d", h=GH)
                    link(dve.tensor_tensor(y, oc[:, t * COLS:(t + 1) * COLS].rearrange("p (h d) -> p h d", h=GH),
                                           spread(stat[:, 8 + 4 * t:12 + 4 * t], GDV), ALU.mult))
                    link(dve.tensor_tensor(y, y, repeat(gnorm[:, l], GH), ALU.mult))
                for at0, c, w in ((0, C_Q, 1024), (1024, C_SU, COLS), (1536, C_CV, COLS)):
                    z = proj[:, :, C_Z + at0:C_Z + at0 + w]
                    a = dve.tensor_tensor(z, z, proj[:, :, c:c + w], ALU.mult)
                a.then_inc(S.y_ready, 1)
                job = jobs[f"out{l}"]
                stream(job, first_tile(job, KC // 2, hT_hi, hT_lo), 1)
                dve.wait_ge(S.act_evacuated, job.E + 4)
                link(dve.tensor_reduce(stat[:, 0:2], stat[:, 16:24].rearrange("p (t n) -> p t n", t=TOK), AX.X, ALU.add))
                variance([(0, 2, D)])
                rstd()
                for t in range(TOK):
                    o = out_sb[:, t, 0:D]
                    link(dve.scalar_tensor_tensor(out=o, in0=o, scalar=stat[:, 8 + t:9 + t], in1=gp[:], op0=ALU.mult, op1=ALU.mult))
                    a = dve.tensor_tensor(x[:, t], x[:, t], o, ALU.add)
                    if t == 0:
                        link(a)
                a.then_inc(S.x_ready, 1)
                dve.wait_ge(S.x_ready, l + 1)

            for l in range(DEPTH):
                lam_init = 0.8 - 0.6 * math.exp(-0.3 * l)
                mean_squares([(0, 2, D)], 2)
                job = jobs[f"c2{l}"]
                stream(job, first_tile(job, KC // 2, hT_hi, hT_lo), 1)
                stream(jobs[f"kr{l}"])
                stream(jobs[f"in2{l}"])
                mean_squares([(0, 2, C_CKV), (2, 4, C_KR - C_CKV)], 4)
                job = jobs[f"uq{l}"]
                stream(job, first_tile(job, 2, cT_hi, cT_lo), 1)
                stream(jobs[f"ukv{l}"])
                dve.wait_ge(S.rows_landed, rows_value(2, l) - 16)
                link(dve.tensor_tensor(lamt[:], lam4[:, 0:2], lam4[:, 2:4], ALU.mult))
                dve.tensor_reduce(stat[:, 48:50], lamt[:], AX.X, ALU.add).then_inc(S.lam_in, 1)
                dve.wait_ge(S.act_evacuated, jobs[f"ukv{l}"].E + 4)
                tmp = [rt[:, i // 2, (i % 2) * 2 * P:(i % 2 + 1) * 2 * P] for i in range(4)]
                for t in range(TOK):
                    q = qm[:, t].rearrange("p (h d) -> p h d", h=HA)
                    cos, sin = K["cos2"][:, 32 * t:32 * t + 32], K["sin2"][:, 32 * t:32 * t + 32]
                    link(rotate(lambda a, b: q[:, :, NOPE + a:NOPE + b], repeat(cos, HA), repeat(sin, HA), 32,
                                [v.rearrange("p (h n) -> p h n", h=HA) for v in tmp]))
                    a = rotate(lambda a, b: proj2[:, t, C_KR + a:C_KR + b], cos, sin, 32, [v[:, 0:32] for v in tmp])
                    if t == 0:
                        link(a)
                a.then_inc(S.rotated, 1)
                attention(mla, l)
                dve.wait_ge(S.lam_exp, l + 1)
                link(dve.tensor_scalar(stat[:, 52:53], stat[:, 48:49], stat[:, 49:50], lam_init, ALU.subtract, ALU.add))
                dve.wait_ge(S.rows_landed, rows_value(2, l))
                attention(dif, l)
                yd = [y2[:, t, HA * VA:HA * VA + 4 * P].rearrange("p (h d) -> p h d", h=4) for t in range(TOK)]
                for t in range(TOK):
                    sq = probs2[:, t].rearrange("p (h d) -> p h d", h=4)
                    link(dve.tensor_tensor(sq, yd[t], yd[t], ALU.mult))
                    link(dve.tensor_reduce(stat[:, 4 * t:4 * t + 4], sq, AX.X, ALU.add))
                variance([(0, 8, P)])
                rstd()
                for t in range(TOK):
                    link(dve.tensor_tensor(yd[t], yd[t], spread(stat[:, 8 + 4 * t:12 + 4 * t], P), ALU.mult))
                    link(dve.scalar_tensor_tensor(out=yd[t], in0=yd[t], scalar=1.0 - lam_init, in1=repeat(subln[:], 4),
                                                  op0=ALU.mult, op1=ALU.mult))
                for half in range(2):
                    b = dve_bank()
                    drained(dve.tensor_tensor(bias_c[:, 2 * half:2 * half + 2], ps[:, b].rearrange("p (h k) -> p h k", h=2),
                                              repeat(K["chunk"], 2), ALU.add))
                attention(chk, l)
                job = jobs[f"o2{l}"]
                prev = stream(job, first_tile(job, KC // 2, hT_hi, hT_lo), 1)
                evacuate(*prev)
                mean_squares([(0, 2, D)], 2)

                def turned(i):
                    for half in range(2):
                        b = dve_bank()
                        k = slice(4 * i + 2 * half, 4 * i + 2 * half + 2)
                        h_, l_ = (u[:, k].rearrange("p c n -> p (c n)") for u in (uT_hi, uT_lo))
                        dve.tensor_scalar(h_, ps[:, b], 1.0, None, ALU.mult).then_inc(S.uT_ready, 1)
                        dve.wait_ge(S.uT_ready, n(S.uT_ready))
                        drained(dve.tensor_tensor(l_, ps[:, b], h_.bitcast(F32), ALU.subtract))
                prev = None
                for h in range(2):
                    up, down = jobs[f"up{l}{h}"], jobs[f"down{l}{h}"]
                    for i in range(up.tiles):
                        if h == 0 and i == 0:
                            first_tile(up, KC // 2, hT_hi, hT_lo)
                        else:
                            lo(up, i, slice(0, 2))
                            if prev:
                                evacuate(*prev)
                                prev = None
                            lo(up, i, slice(2, None))
                        if i:
                            turned(i - 1)
                    turned(up.tiles - 1)
                    prev = stream(down)
                evacuate(*prev)
            mean_squares([(0, 2, D)], 2)
            rstd()
            dve.wait_ge(S.rows_landed, 16 * (ROWS1 * DEPTH + ROWS2 * DEPTH + 1))
            for t in range(TOK):
                link(dve.tensor_scalar(fout[:, t], x[:, t], stat[:, 8 + t:9 + t], None, ALU.mult))
                dve.tensor_tensor(fout[:, t], fout[:, t], frow[:], ALU.mult).then_inc(S.final_ready, 1)

        @block.tensor
        def _(pe):
            n = Tally()

            def act_bank():
                u = n(S.act_bank_filled) - 1
                if u >= 2:
                    pe.wait_ge(S.act_bank_drained, u - 1)
                return 6 + u % 2

            def dve_bank():
                u = n(S.dve_bank_filled) - 1
                if u >= 2:
                    pe.wait_ge(S.dve_bank_drained, u - 1)
                return 4 + u % 2

            def act_done():
                pe.wait_ge(S.act_bank_drained, n.so_far(S.act_bank_filled))

            def dve_done():
                pe.wait_ge(S.dve_bank_drained, n.so_far(S.dve_bank_filled))

            def transposes(sources, rows=P):
                b = act_bank()
                for j, s in enumerate(sources):
                    mm = pe.transpose(ps[0:rows, b, j * P:(j + 1) * P], s, ident)
                mm.then_inc(S.act_bank_filled, 1)

            def multiply(job, i, js):
                hi, lo = job.lhs
                for j, G, L, k0, cnt in list(groups(job, i))[js]:
                    T = job.T + i
                    if j == 0 and T >= 2:
                        before = next(b for b in order if b.T <= T - 2 < b.T + b.tiles)
                        pe.wait_ge(S.act_evacuated if before.evac == "act" else S.dve_evacuated,
                                   before.E + T - 2 - before.T + 1)
                    pe.wait_ge(S.group_read, G + 1)
                    s = L % SPLIT_SLOTS
                    for c in range(cnt):
                        wh, wl = (w[:, s, c * job.width:(c + 1) * job.width] for w in (w_hi, w_lo))
                        k = job.lhs0 + k0 + c
                        for t in range(TOK):
                            o = ps[:, bank(job, i, t), 0:job.width]
                            a, b = (v[:, k, t * P:(t + 1) * P] for v in (hi, lo))
                            pe.matmul(o, a, wh, start=k0 + c == 0, stop=False)
                            pe.matmul(o, a, wl, start=False, stop=False)
                            mm = pe.matmul(o, b, wh, start=False, stop=k0 + c == job.chunks - 1)
                    mm.then_inc(S.group_multiplied, 1)

            def first_tile(job, src, col=lambda c: c * P):
                chunks = job.chunks if job.chunks == KC else 4
                banks = chunks // 2

                def turn(b):
                    transposes([src[:, t, col(c):col(c) + P] for c in (2 * b, 2 * b + 1) for t in range(TOK)])
                turn(0)
                turn(1)
                for j in range(max(banks, len(job.groups))):
                    if j + 2 < banks:
                        turn(j + 2)
                    if j < banks:
                        pe.wait_ge(S.lhs_ready, n(S.lhs_ready))
                    if j < len(job.groups):
                        multiply(job, 0, slice(j, j + 1))

            def product(job, start=0):
                for i in range(start, job.tiles):
                    multiply(job, i, slice(None))

            def attention(m):
                for dst, sources, rows in m.prep:
                    transposes(sources, rows)

                def scores(g):
                    t, hs = m.groups[g]
                    nk = (t + 1) * P
                    b = dve_bank()
                    for j, h in enumerate(hs):
                        parts = m.qk(h)
                        for a, (q, k) in enumerate(parts):
                            mm = pe.matmul(ps[:, b, j * nk:(j + 1) * nk], q[:, t * P:(t + 1) * P], k[:, 0:nk],
                                           start=a == 0, stop=a == len(parts) - 1)
                    mm.then_inc(S.dve_bank_filled, 1)
                act_done()
                scores(0)
                for g, (t, hs) in enumerate(m.groups):
                    if g + 1 < len(m.groups):
                        scores(g + 1)
                    pe.wait_ge(S.probs_ready, n(S.probs_ready))
                    transposes([m.probs[:, g % 2, j * P:(j + 1) * P] for j in range(4)])
                    b = dve_bank()
                    act_done()
                    for j, h in enumerate(hs):
                        for kk in range(t + 1):
                            i = j * (t + 1) + kk
                            mm = pe.matmul(ps[:, b, j * m.dv:(j + 1) * m.dv], m.probsT[:, g % 2, i * P:(i + 1) * P],
                                           m.v(h, kk), start=kk == 0, stop=kk == t)
                    mm.then_inc(S.dve_bank_filled, 1)

            pe.wait_ge(S.const_landed, 48)
            pe.wait_ge(S.small_landed, 16 * 6)
            for l in range(DEPTH):
                for t in range(MOD_TILES):
                    pe.wait_ge(S.group_read, mod_at[l] + (t + 1) * MOD_GROUPS)
                    b = dve_bank()
                    if t < 8:
                        for j in range(4):
                            for a in range(2):
                                mm = pe.matmul(ps[:, b, j:j + 1], acc[:, t % 2, a, j * P:(j + 1) * P],
                                               K["ones"][:, 0:1], start=a == 0, stop=a == 1)
                    else:
                        for a in range(2):
                            mm = pe.matmul(ps[:, b], K["ones"], acc[:, t % 2, a], start=a == 0, stop=a == 1)
                    mm.then_inc(S.dve_bank_filled, 1)
                pe.wait_ge(S.xn_ready, l + 1)
                first_tile(jobs[f"in{l}"], xn)
                product(jobs[f"in{l}"], 1)
                product(jobs[f"cg{l}"])
                product(jobs[f"z{l}"])
                pe.wait_ge(S.act_evacuated, jobs[f"z{l}"].E + 4)
                pe.wait_ge(S.rotated, n(S.rotated))
                attention(swa)
                pe.wait_ge(S.rows_landed, rows_value(1, l))
                for half in range(2):
                    b = dve_bank()
                    for j in range(4):
                        mm = pe.transpose(ps[:, b, j * P:(j + 1) * P], sgw[:, 4 * half + j], ident)
                    mm.then_inc(S.dve_bank_filled, 1)
                dve_done()
                for half in range(2):
                    b = dve_bank()
                    for j in range(4):
                        g = 4 * half + j
                        mm = pe.matmul(ps[:, b, j * P:(j + 1) * P].rearrange("p (n c) -> p n c", n=TOK), sgwT[:, g],
                                       proj[:, :, C_SV + g * SGD:C_SV + (g + 1) * SGD], start=True, stop=True)
                    mm.then_inc(S.dve_bank_filled, 1)
                transposes([proj[:, t, C_CG:C_CG + RANK] for t in range(TOK)], RANK)
                for c in (C_CQ, C_CK):
                    transposes([proj[:, t, c + kt * P:c + (kt + 1) * P] for kt in range(2) for t in range(TOK)])
                b = dve_bank()
                act_done()
                for kt in range(2):
                    mm = pe.matmul(ps[:, b, kt * 2 * P:(kt + 1) * 2 * P], gup[:, l, kt * P:(kt + 1) * P], cgT[:],
                                   start=True, stop=True)
                mm.then_inc(S.dve_bank_filled, 1)
                for lev in range(LEVELS + 2):
                    q, k = gq[:, 0], gq[:, 1]
                    if lev:
                        pe.wait_ge(S.gla_q, n(S.gla_q))
                        pe.wait_ge(S.gla_k, n(S.gla_k))
                        q, k = qlev[:, lev % 2], klev[:, lev % 2]
                    for ts, tt in (((0, 0), (1, 1)) if lev <= LEVELS else ((0, 1),)):
                        b = dve_bank()
                        for h in (0, 2, 1, 3):
                            r = (h % 2) * GDK
                            if h == 1:
                                mm.then_inc(S.pe_step, 1)
                                pe.wait_ge(S.pe_step, n(S.pe_step))
                            mm = pe.matmul(ps[:, b, h * P:(h + 1) * P], k[r:r + GDK, h // 2, ts * P:(ts + 1) * P],
                                           q[r:r + GDK, h // 2, tt * P:(tt + 1) * P], start=True, stop=True)
                        mm.then_inc(S.dve_bank_filled, 1)
                dve_done()
                for t in range(TOK):
                    b = dve_bank()
                    terms = [(0, 0)] if t == 0 else [(1, 1), (2, 0)]
                    for h in range(GH):
                        for a, (i, sv) in enumerate(terms):
                            mm = pe.matmul(ps[:, b, h * P:(h + 1) * P], pairs[:, i, h * P:(h + 1) * P],
                                           proj[:, sv, C_CV + h * P:C_CV + (h + 1) * P],
                                           start=a == 0, stop=a == len(terms) - 1)
                    mm.then_inc(S.dve_bank_filled, 1)
                pe.wait_ge(S.y_ready, l + 1)
                first_tile(jobs[f"out{l}"], proj, lambda c: C_Z + c * P)
                product(jobs[f"out{l}"], 1)
            for l in range(DEPTH):
                x_complete(pe, l, 0)
                first_tile(jobs[f"c2{l}"], x)
                product(jobs[f"kr{l}"])
                product(jobs[f"in2{l}"])
                pe.wait_ge(S.act_evacuated, jobs[f"in2{l}"].E + 6)
                first_tile(jobs[f"uq{l}"], proj2)
                product(jobs[f"uq{l}"], 1)
                product(jobs[f"ukv{l}"])
                pe.wait_ge(S.act_evacuated, jobs[f"ukv{l}"].E + 4)
                pe.wait_ge(S.rotated, n(S.rotated))
                attention(mla)
                attention(dif)
                pe.wait_ge(S.rows_landed, rows_value(2, l))
                for half in range(2):
                    b = dve_bank()
                    pe.matmul(ps[:, b], K["flip"], bias_c[:, 2 * half:2 * half + 2].rearrange("p h k -> p (h k)"),
                              start=True, stop=True).then_inc(S.dve_bank_filled, 1)
                attention(chk)
                dve_done()
                first_tile(jobs[f"o2{l}"], y2)
                product(jobs[f"o2{l}"], 1)
                x_complete(pe, l, 1)

                def turn_u(i):
                    pe.wait_ge(S.u_ready, n(S.u_ready))
                    for c0 in (0, 2):
                        b = dve_bank()
                        for a in range(4):
                            c = c0 + a // 2
                            mm = pe.transpose(ps[:, b, a * P:(a + 1) * P], u_nat[:, i % 2, a % 2, c * P:(c + 1) * P], ident)
                        mm.then_inc(S.dve_bank_filled, 1)
                for h in range(2):
                    up, down = jobs[f"up{l}{h}"], jobs[f"down{l}{h}"]
                    for i in range(up.tiles):
                        if h == 0 and i == 0:
                            first_tile(up, x)
                            continue
                        multiply(up, i, slice(0, 4))
                        if i:
                            turn_u(i - 1)
                        multiply(up, i, slice(4, None))
                    turn_u(up.tiles - 1)
                    dve_done()
                    product(down)


_INPUTS = ("x", "w_mod", "b_mod", "g_post", "w_in", "w_out", "swa_sinks", "sg_w", "sg_ln_g", "sg_ln_b",
           "gla_w_gate_up", "gla_norm_g", "w_in_2", "w_uq_2", "w_ukv_2", "w_o_2", "w_up_2", "w_down_2",
           "diff_subln_2", "final_norm_2")


def columns(v):
    return v.reshape(v.shape[0], -1, P).transpose(2, 0, 1)


def kernel(**inputs):
    import concourse.bacc as bacc
    from concourse.bass_utils import run_bass_kernel_spmd as run

    a = {k: np.asarray(v) for k, v in inputs.items()}
    const, levels, diff = constants()
    arrays = {k: a[k] for k in _INPUTS}
    arrays["c"] = a["c"].reshape(KC, P).T
    arrays["positions"] = a["positions"].reshape(TOK, P).T
    arrays["cols1"] = np.concatenate([columns(a["g_pre"]), columns(a["b_mod"]), a["sg_b"].transpose(2, 0, 1),
                                      columns(a["gla_b_gate"])], axis=2)
    arrays["cols2"] = np.concatenate([columns(a[k]) for k in ("attn_norm_2", "mlp_norm_2", "q_a_norm_2", "kv_a_norm_2")], axis=2)
    arrays["lambdas"] = np.stack([a[k] for k in ("lambda_q1_2", "lambda_q2_2", "lambda_k1_2", "lambda_k2_2")], axis=1)
    arrays["rel"] = np.concatenate([a["rel_bias_2"][:, :, ::-1],
                                    np.zeros((DEPTH, 4, REL_PAD - REL), np.float32)], axis=2)
    arrays["const"], arrays["levels"], arrays["diff_bias"] = const, levels, diff

    nc = bacc.Bacc("TRN2", target_bir_lowering=False, num_devices=1)
    io, sent = {}, {}
    for name, v in arrays.items():
        v = np.ascontiguousarray(v)
        sent[f"in_{name}"] = v
        io[name] = nc.dram_tensor(f"in_{name}", v.shape, mybir.dt.from_np(v.dtype), kind="ExternalInput").ap()
    io["out"] = nc.dram_tensor("out_0", (1, TOK * P, D), F32, kind="ExternalOutput").ap()
    build(nc, io)
    return run(nc, [sent], core_ids=[0]).results[0]["out_0"]
```

```python
from contextlib import ExitStack
import math

import numpy as np

import concourse.bass as bass
from concourse import mybir

F32 = mybir.dt.float32
F32R = mybir.dt.float32r
I32 = mybir.dt.int32
ACT = mybir.ActivationFunctionType
ALU = mybir.AluOpType
AX = mybir.AxisListType

P = 128
TOK = 2
D = 2048
KC = D // P
DEPTH = 2
EPS = 1e-6
BIG = 1e30
RAW_SLOTS = 6
SPLIT_SLOTS = 4
AHEAD = 2
GROUP = 1024
COLS = 512

HD = 64
QH, KVH = 16, 4
C_Q, C_K, C_V, C_SU, C_SV, C_CQ, C_CK, C_CV, C_CG, C_Z = 0, 1024, 1280, 1536, 2048, 2560, 2816, 3072, 3584, 3600
W1 = 5648
SGG, SGD = 8, 64
GH, GDK, GDV, RANK = 4, 64, 128, 16
LEVELS = 7
HALF = 8
C_CQ2, C_CKV, C_KR, C_QB, C_KB, C_VB, C_QC, C_KC, C_VC = 0, 384, 512, 576, 1088, 1600, 2112, 2624, 3136
W2 = 3648
HA, NOPE, ROPE, VA = 8, 128, 64, 128
DFF = 4 * D
UPC = 4096
REL = 320
REL_PAD = 384

CONST_COLS = {}
ROUND = 1.5 * 2 ** 23
TWO_PI = (6.28125, 2029.0 / 2 ** 20, 2 * np.pi - 6.28125 - 2029.0 / 2 ** 20)
PI_BELOW = 3.1415925
_at = 0
for _name, _n in (("ident", 128), ("flip", 128), ("ones", 128), ("swa", 256), ("chunk", 256), ("tril", 128),
                  ("inv_freq", HALF), ("cos2", 64), ("sin2", 64)):
    CONST_COLS[_name] = (_at, _n)
    _at += _n
CONST_W = _at


def constants():
    q = np.arange(P)[:, None]
    k = np.arange(2 * P)[None, :]
    c = np.zeros((P, CONST_W), np.float32)

    def put(name, v):
        a, n = CONST_COLS[name]
        c[:, a:a + n] = v
    put("ident", np.eye(P))
    put("flip", np.eye(P)[::-1])
    put("ones", 1.0)
    dist = q + P - k
    put("swa", np.where((dist >= 0) & (dist < P), 0.0, -BIG))
    put("chunk", np.where(k // 64 <= (q + P) // 64, 0.0, -BIG))
    put("tril", (q <= np.arange(P)[None, :]))
    f1 = np.float32(500000.0) ** (-(np.arange(HALF, dtype=np.float32) * np.float32(2.0 / 16)))
    put("inv_freq", f1[None, :])
    f2 = np.float32(10000.0) ** (-np.arange(32, dtype=np.float32) / np.float32(32))
    ang = np.arange(2 * P, dtype=np.float32)[:, None] * f2[None, :]
    lay = lambda v: v.reshape(2, P, 32).transpose(1, 0, 2).reshape(P, 64)
    put("cos2", lay(np.cos(ang.astype(np.float64))))
    put("sin2", lay(np.sin(ang.astype(np.float64))))
    s = np.arange(P)[:, None]
    t = np.arange(P)[None, :]
    lv = [s == t]
    for n in range(1, LEVELS + 1):
        b = 2 ** n
        lv.append((s // b == t // b) & (s % b < b // 2) & (t % b >= b // 2))
    levels = np.concatenate([m.astype(np.int32) for m in lv], axis=1)
    slopes = (2.0 ** (-8.0 * (np.arange(4, dtype=np.float32) + 1.0) / 4)).astype(np.float32)
    d2 = np.abs(q + P - k).astype(np.float32)
    ok = k // 64 <= (q + P) // 64
    diff = np.concatenate([np.where(ok, -sl * d2, -BIG).astype(np.float32) for sl in slopes], axis=1)
    return c, levels, diff


class Tally:

    def __init__(self):
        self.n = {}

    def __call__(self, sem, by=1):
        self.n[sem.name] = self.n.get(sem.name, 0) + by
        return self.n[sem.name]

    def so_far(self, sem):
        return self.n.get(sem.name, 0)


class Job:

    def __init__(self, name, w, chunks, ncols, width, lhs, col0=0, lhs0=0, evac="act"):
        self.name, self.w, self.chunks, self.width, self.lhs = name, w, chunks, width, lhs
        self.kind = name.rstrip("01")
        self.layer = int(name[len(self.kind)])
        self.tiles = ncols // width
        self.col0, self.lhs0, self.evac = col0, lhs0, evac
        per = max(1, GROUP // width) if width >= 256 else chunks
        self.groups = [(k, min(per, chunks - k)) for k in range(0, chunks, per)]


def build(nc, io):
    ctx = ExitStack()
    with ctx:
        cursor = [(nc.sbuf_base + 63) // 64 * 64]
        made = {}

        def at(name, shape, dt, offset):
            made[name] = nc.alloc_sbuf_tensor_at(name, shape, dt, offset=offset)
            return made[name]

        def words(shape):
            return int(np.prod(shape[1:]))

        def sb(name, shape, dt=F32):
            t = at(name, shape, dt, cursor[0])
            cursor[0] += (4 * words(shape) + 31) // 32 * 32
            return t

        class Area:

            def __init__(self, start):
                self.start = self.end = start

            def __call__(self, name, shape, dt=F32):
                t = at(name, shape, dt, self.end)
                self.end += (4 * words(shape) + 31) // 32 * 32
                return t

        x = sb("x", [P, TOK, D])
        hT_at = cursor[0]
        hT_hi = sb("hT_hi", [P, KC, 2 * P], F32R)
        hT_lo = sb("hT_lo", [P, KC, 2 * P], F32R)
        raw = sb("raw", [P, RAW_SLOTS, GROUP])
        w_hi = sb("w_hi", [P, SPLIT_SLOTS, GROUP], F32R)
        w_lo = sb("w_lo", [P, SPLIT_SLOTS, GROUP], F32R)
        hf_at = cursor[0]
        hf = sb("hf", [P, 2, 2, 2 * P])
        cst = sb("cst", [P, CONST_W])
        K = {n: cst[:, a:a + w] for n, (a, w) in CONST_COLS.items()}
        ident = K["ident"]
        cols1 = sb("cols1", [P, DEPTH, 90])
        mod = sb("mod", [P, DEPTH, 3 * KC])
        cols2 = sb("cols2", [P, DEPTH, 36])
        c_col = sb("c_col", [P, KC])
        minus_half = sb("minus_half", [P, 8])
        stat = sb("stat", [P, 64])
        cs1 = sb("cs1", [P, 2, TOK, HALF])
        turns = sb("turns", [P, TOK * HALF])
        bn = sb("bn", [P, TOK, 6])
        smax = sb("smax", [P, 3, 4])
        ssum = sb("ssum", [P, 3, 4])
        sden = sb("sden", [P, 3, 4])
        srec = sb("srec", [P, 3, 4])
        ses = sb("ses", [P, 3, 4])
        work_at = cursor[0]

        A1 = Area(work_at)
        proj = A1("proj", [P, TOK, W1])
        sinks = A1("sinks", [P, DEPTH, QH])
        neg_sinks = A1("neg_sinks", [P, DEPTH, QH])
        gnorm = A1("gnorm", [P, DEPTH, GDV])
        gup = A1("gup", [RANK, DEPTH, GH * GDK])
        hcol = A1("hcol", [P, KC])
        gcol = A1("gcol", [P, KC])
        acc = A1("acc", [P, 2, 2, COLS])
        levels = A1("levels", [P, LEVELS + 1, P], I32)
        glx = A1("glx", [P, 2, 2 * P])
        glb = A1("glb", [P, 2, 2 * P])
        diag = [v[:].rearrange("p k n -> p (k n)") for v in (glx, glb)]
        keys2 = diag
        rotation_tmp = [v[:, i, 0:(QH + KVH) * HALF] for v in (glx, glb) for i in range(2)]
        cgT = A1("cgT", [RANK, 2 * P])
        A1g = Area(A1.end)
        probs = A1("probs", [P, 2, COLS])
        probsT = A1("probsT", [P, 2, COLS])
        gle = A1g("gle", [P, 2, 2, 2 * P])
        glf = A1g("glf", [P, 2, 2, 2 * P])
        A1k = Area(A1.end)
        q1T = A1("q1T", [P, QH // 2, 2 * P])
        k1T = A1("k1T", [P, KVH, 2 * P])
        A1s = Area(A1k.end)
        sgwT = A1s("sgwT", [P, SGG, P])
        sgw = A1("sgw", [P, SGG, P])
        sgln = A1("sgln", [P, 2, COLS])
        gq = A1k("gq", [P, 2, 2, 2 * P])
        qlev = A1k("qlev", [P, 2, 2, 2 * P])
        klev = A1k("klev", [P, 2, 2, 2 * P])
        pairs = A1k("pairs", [P, 3, COLS])
        xn = proj
        gp = [proj[:, i // 2, D + i % 2 * COLS:D + (i % 2 + 1) * COLS] for i in range(4)]
        out_sb = proj
        oc = gle[:, :, :, :].rearrange("p a b n -> p (a b n)")
        osq = glf[:, :, :, :].rearrange("p a b n -> p (a b n)")

        A2 = Area(work_at)
        proj2 = A2("proj2", [P, TOK, W2])
        qm = A2("qm", [P, TOK, HA * (NOPE + ROPE)])
        y_mla = qm[:, :, 0:HA * VA]
        kv_at = A2.end
        kv = A2("kv", [P, TOK, HA * (NOPE + VA)])
        probs2 = A2("probs2", [P, 2, COLS])
        probs2T = A2("probs2T", [P, 2, COLS])
        bias_d = A2("bias_d", [P, 4, 2 * P])
        A2q = Area(A2.end)
        cT_hi = A2("cT_hi", [P, 4, 2 * P], F32R)
        cT_lo = A2("cT_lo", [P, 4, 2 * P], F32R)
        qrT = A2q("qrT", [ROPE, HA, 2 * P])
        krT = at("krT", [ROPE, 2 * P], F32, hf_at)
        A2k = Area(A2.end)
        kaT = A2("kaT", [P, HA, 2 * P])
        rt = A2k("rt", [P, 2, COLS])
        lam4 = A2k("lam4", [P, 4, HD])
        lamt = A2k("lamt", [P, 2, HD])
        qaT = A2("qaT", [P, HA, 2 * P])
        A2v = Area(kv_at)
        bias_c = A2v("bias_c", [P, 4, 2 * P])
        subln = A2v("subln", [P, P])
        dtmp = A2v("dtmp", [P, 2, P])
        A2m = Area(work_at)
        u_nat = A2m("u_nat", [P, 2, TOK, COLS])
        uT_hi = A2m("uT_hi", [P, UPC // P, 2 * P], F32R)
        uT_lo = A2m("uT_lo", [P, UPC // P, 2 * P], F32R)
        junk_m = A2m("junk_m", [P, COLS])
        A3 = Area(work_at)
        frow = A3("frow", [P, D])
        fout = A3("fout", [P, TOK, D])
        for area, end in ((A1, nc.sbuf_usable_end), (A2, nc.sbuf_usable_end), (A2m, nc.sbuf_usable_end),
                          (A1k, A1.end), (A2v, kv_at + 4 * 2 * HA * (NOPE + VA))):
            assert area.end <= end, (area.start, area.end, end)

        ps = ctx.enter_context(nc.psum_tensor("ps", [P, 8, COLS], F32))

        def sem(name):
            return ctx.enter_context(nc.semaphore(name))

        raw_landed = [sem(f"raw_landed{i}") for i in range(RAW_SLOTS)]
        class S:
            x_landed = sem("x_landed")
            const_landed = sem("const_landed")
            small_landed = sem("small_landed")
            rows_landed = sem("rows_landed")
            out_stored = sem("out_stored")
            hi_ready = sem("hi_ready")
            group_read = sem("group_read")
            group_multiplied = sem("group_multiplied")
            act_evacuated = sem("act_evacuated")
            dve_evacuated = sem("dve_evacuated")
            act_bank_filled = sem("act_bank_filled")
            act_bank_drained = sem("act_bank_drained")
            dve_bank_filled = sem("dve_bank_filled")
            dve_bank_drained = sem("dve_bank_drained")
            act_step = sem("act_step")
            dve_step = sem("dve_step")
            pool_step = sem("pool_step")
            pe_step = sem("pe_step")
            lhs_hi = sem("lhs_hi")
            lhs_ready = sem("lhs_ready")
            squares_ready = sem("squares_ready")
            var_ready = sem("var_ready")
            rstd_ready = sem("rstd_ready")
            rotated = sem("rotated")
            neg_max_ready = sem("neg_max_ready")
            probs_ready = sem("probs_ready")
            hcol_ready = sem("hcol_ready")
            gla_factor = sem("gla_factor")
            gla_q = sem("gla_q")
            gla_k = sem("gla_k")
            gla_logits = sem("gla_logits")
            gla_ln = sem("gla_ln")
            gla_dist = sem("gla_dist")
            xn_ready = sem("xn_ready")
            y_ready = sem("y_ready")
            x_ready = sem("x_ready")
            u_ready = sem("u_ready")
            uT_ready = sem("uT_ready")
            lam_in = sem("lam_in")
            lam_exp = sem("lam_exp")
            tables = sem("tables")
            final_ready = sem("final_ready")
            mla_done = sem("mla_done")
            yd_ready = sem("yd_ready")
            mod_ready = sem("mod_ready")
            v_ready = sem("v_ready")
            diag_ready = sem("diag_ready")
            ang_ready = sem("ang_ready")

        jobs = {}
        order = []
        state = dict(G=0, L=0, T=0, act=0, dve=0)
        loads = []
        group_at = []
        mods_at = {}
        mod_sums = {}

        def mod_group(l, t, g):
            loads.append((io["w_mod"][l, 2 * g * P:2 * (g + 1) * P, t * COLS:(t + 1) * COLS], 2, COLS))
            return l, t, g, len(loads) - 1

        def plan(*parts, mods=()):
            steps = []
            for job, num, den in parts:
                job.L, job.T = state["L"] + len(steps), state["T"]
                job.E = state[job.evac]
                n = job.tiles * len(job.groups)
                steps += [(job, q, (q + 1) * num // den - q * num // den) for q in range(n)]
                state["T"] += job.tiles
                state[job.evac] += job.tiles
                jobs[job.name] = job
                order.append(job)
            loaded = 0
            for step, (_, _, times) in enumerate(steps):
                L = state["L"] + step
                for _ in range(times):
                    if mods:
                        l, t, g = mods.pop(0)
                        mods_at.setdefault(L, []).append(mod_group(l, t, g))
                        if g == MOD_GROUPS - 1:
                            mod_sums[L + 3] = (l, t)
                while loaded <= min(step + AHEAD, len(steps) - 1):
                    job, q, _ = steps[loaded]
                    i, (k0, cnt) = q // len(job.groups), job.groups[q % len(job.groups)]
                    c0 = job.col0 + i * job.width
                    loads.append((job.w[k0 * P:(k0 + cnt) * P, c0:c0 + job.width], cnt, job.width))
                    group_at.append(len(loads) - 1)
                    loaded += 1
            state["L"] += len(steps)

        MOD_TILES = 3 * D // COLS
        MOD_GROUPS = KC // 2
        hT = (hT_hi, hT_lo)
        mods_first = [mod_group(0, t, g) for t in range(8) for g in range(MOD_GROUPS)]
        mods = [(0, t, g) for t in range(8, MOD_TILES) for g in range(MOD_GROUPS)]
        for l in range(DEPTH):
            w = io["w_in"][l]
            if l + 1 < DEPTH:
                mods += [(l + 1, t, g) for t in range(MOD_TILES) for g in range(MOD_GROUPS)][:8 * MOD_GROUPS]
            else:
                mods += [(l, t, g) for t in range(8, MOD_TILES) for g in range(MOD_GROUPS)]
            rest = C_Z - 3 * COLS
            plan((Job(f"in{l}", w, KC, 3 * COLS, COLS, hT), 1, 1),
                 (Job(f"rest{l}", w, KC, rest, rest // 6, hT, col0=3 * COLS), 1, 2),
                 (Job(f"z{l}", w, KC, D, COLS, hT, col0=C_Z), 6, 8), mods=mods)
            plan((Job(f"out{l}", io["w_out"][l], KC, D, COLS, hT), 1, 1), mods=mods)
            assert not mods
        for l in range(DEPTH):
            w = io["w_in_2"][l]
            tile = W2 // 8
            plan((Job(f"c2{l}", w, KC, 2 * tile, tile, hT), 0, 1),
                 (Job(f"in2{l}", w, KC, tile, tile, hT, col0=2 * tile), 0, 1))
            plan((Job(f"uq{l}", io["w_uq_2"][l], 3, HA * (NOPE + ROPE), COLS, (cT_hi, cT_lo)), 0, 1),
                 (Job(f"ukv{l}", io["w_ukv_2"][l], 1, HA * (NOPE + VA), COLS, (cT_hi, cT_lo), lhs0=3), 0, 1))
            plan((Job(f"rest2{l}", w, KC, 5 * tile, tile, hT, col0=3 * tile), 0, 1))
            for name, k0, cnt in (("oa", 0, 8), ("ob", 8, 4), ("oc", 12, 4)):
                plan((Job(f"{name}{l}", io["w_o_2"][l, k0 * P:(k0 + cnt) * P], cnt, D, COLS, hT, lhs0=k0, evac="dve"), 0, 1))
            plan(*[part for h in range(2) for part in (
                (Job(f"up{l}{h}", io["w_up_2"][l], KC, UPC, COLS, hT, col0=h * UPC), 0, 1),
                (Job(f"down{l}{h}", io["w_down_2"][l, h * UPC:(h + 1) * UPC], UPC // P, D, COLS,
                     (uT_hi, uT_lo), evac="dve"), 0, 1))])

        def each_group(jobs_):
            for job in jobs_:
                for i in range(job.tiles):
                    for j in range(len(job.groups)):
                        yield job, i, j, job.L + i * len(job.groups) + j

        def ahead(jobs_):
            groups = list(each_group(jobs_))
            upto = 0
            for q, group in enumerate(groups):
                end = min(q + AHEAD + 1, len(groups))
                yield (*group, [(job, j, L) for job, i, j, L in groups[upto:end]])
                upto = end

        def count(jobs_):
            return sum(job.tiles * len(job.groups) for job in jobs_) + 1

        def take(steps, k):
            for _ in range(k):
                next(steps)

        def finish(steps):
            for _ in steps:
                pass

        def share(total, slots):
            return [(s + 1) * total // slots - s * total // slots for s in range(slots)]

        def interleave(wide, total, mixer, slots):
            for k in share(total, slots):
                take(wide, k)
                next(mixer)
            finish(mixer)

        def bank(job, i, t):
            return 2 * ((job.T + i) % 2) + t

        def tile_multiplied(job, i):
            return job.L + (i + 1) * len(job.groups)


        block = ctx.enter_context(nc.Block())

        class Mixer:

            def __init__(self, heads, dk, dv, scale, probs, probsT, parity=1):
                self.heads, self.dk, self.dv, self.scale, self.probs, self.probsT = heads, dk, dv, scale, probs, probsT
                self.groups = []
                for t, size in ((0, 4), (1, 2)):
                    step = size * parity
                    self.groups += [(t, list(range(h + p, h + p + step, parity)))
                                    for h in range(0, heads, step) for p in range(parity)]

            def slots(self):
                return (len(self.prep) + 1) // 2 + len(self.groups) + 2

        def repeat(ap, times):
            return ap.unsqueeze(1).broadcast_to([ap.shape[0], times, ap.shape[-1]])

        def spread(ap, times):
            return ap.unsqueeze(2).broadcast_to([ap.shape[0], ap.shape[-1], times])

        def head_pairs(src, col, stride, width, heads, dst):
            return [(dst[0:width, h:h + 2].rearrange("p h n -> p (h n)"),
                     [src[:, t, col + (h + a) * stride:col + (h + a) * stride + width]
                      for a in range(2) for t in range(TOK)], width) for h in range(0, heads, 2)]

        swa = Mixer(QH, HD, HD, HD ** -0.5, probs, probsT, parity=2)
        swa.qk = lambda h: [(q1T[h % 2 * HD:(h % 2 + 1) * HD, h // 2], k1T[h % 2 * HD:(h % 2 + 1) * HD, h // (QH // KVH)])]
        swa.v = lambda h, kk: proj[:, kk, C_V + (h // 4) * HD:C_V + (h // 4 + 1) * HD]
        swa.prep = head_pairs(proj, C_Q, P, P, QH // 2, q1T)
        swa.prep += [(k1T[:, h:h + 2].rearrange("p h n -> p (h n)"),
                      [keys2[t][:, (h + a) * P:(h + a + 1) * P] for a in range(2) for t in range(TOK)], P)
                     for h in range(0, KVH, 2)]
        swa.masks = lambda t, hs: [(0, len(hs), repeat(K["swa"][:, (1 - t) * P:], len(hs)))]
        swa.out = lambda t, hs: proj[:, t, C_Q:C_K].rearrange("p (h d) -> p h d", d=HD)[:, hs[0]:hs[-1] + 1:2]

        mla = Mixer(HA, P, VA, (NOPE + ROPE) ** -0.5, probs2, probs2T)
        mla.qk = lambda h: [(qaT[:, h], kaT[:, h]), (qrT[:, h], krT[:])]
        mla.v = lambda h, kk: kv[:, kk, h * 256 + NOPE:(h + 1) * 256]
        mla.prep = (head_pairs(qm, 0, 192, NOPE, HA, qaT) + head_pairs(qm, NOPE, 192, ROPE, HA, qrT)
                    + head_pairs(kv, 0, 256, NOPE, HA, kaT)
                    + [(krT[:], [proj2[:, t, C_KR:C_KR + ROPE] for t in range(TOK)], ROPE)])
        mla.masks = lambda t, hs: [(0, len(hs), repeat(K["chunk"][:, (1 - t) * P:], len(hs)))]
        mla.out = lambda t, hs: y_mla[:, t, hs[0] * VA:(hs[-1] + 1) * VA].rearrange("p (h d) -> p h d", d=VA)

        dif = Mixer(8, HD, P, HD ** -0.5, probs2, probs2T)
        dif.qk = lambda u: [(qaT[0:HD, u], kaT[0:HD, u])]
        dif.v = lambda u, kk: proj2[:, kk, C_VB + (u // 2) * P:C_VB + (u // 2 + 1) * P]
        dif.prep = head_pairs(proj2, C_QB, HD, HD, 8, qaT) + head_pairs(proj2, C_KB, HD, HD, 8, kaT)
        dif.masks = lambda t, hs: [(j, j + 2, repeat(bias_d[:, hs[j] // 2, (1 - t) * P:], 2)) for j in range(0, len(hs), 2)]
        dif.out = lambda t, u: proj2[:, t, C_QB + (u // 2) * P:C_QB + (u // 2 + 1) * P]

        chk = Mixer(4, P, P, P ** -0.5, probs2, probs2T)
        chk.qk = lambda h: [(qaT[:, h], kaT[:, h])]
        chk.v = lambda h, kk: proj2[:, kk, C_VC + h * P:C_VC + (h + 1) * P]
        chk.prep = head_pairs(proj2, C_QC, P, P, 4, qaT) + head_pairs(proj2, C_KC, P, P, 4, kaT)
        chk.masks = lambda t, hs: [(0, len(hs), bias_c[:, hs[0]:hs[0] + len(hs), (1 - t) * P:])]
        chk.out = lambda t, hs: proj2[:, t, C_QC + hs[0] * P:C_QC + (hs[-1] + 1) * P].rearrange("p (h d) -> p h d", d=P)

        GLA_SLOTS = 3 + LEVELS + 1 + 3
        MIX1_SLOTS = 1 + swa.slots() + 3 + GLA_SLOTS

        ROWS1 = 3
        ROWS2 = 4

        def rows_value(block, l, part=None):
            if block == 1:
                return 16 * ROWS1 * (l + 1)
            return 16 * (ROWS1 * DEPTH + ROWS2 * l + (2 if part == "first" else ROWS2))

        def rstd_value(l, k):
            return 4 * DEPTH + 4 * l + k + 1

        def x_complete(eng, l, half):
            if half == 1:
                eng.wait_ge(S.dve_evacuated, jobs[f"oc{l}"].E + 4)
            elif l:
                eng.wait_ge(S.dve_evacuated, jobs[f"down{l - 1}1"].E + 4)
            else:
                eng.wait_ge(S.x_ready, 4 * DEPTH)

        @block.sync
        def _(sp):
            sp.dma_start(c_col[:], io["c"]).then_inc(S.const_landed, 16)
            sp.dma_start(cst[:], io["const"]).then_inc(S.const_landed, 16)
            sp.dma_start(cols1[:], io["cols1"]).then_inc(S.const_landed, 16)
            sp.dma_start(x[:], io["x"][0].rearrange("(t p) n -> p t n", p=P)).then_inc(S.x_landed, 16)
            for G, (src, cnt, width) in enumerate(loads):
                slot = G % RAW_SLOTS
                if G >= RAW_SLOTS:
                    sp.wait_ge(S.group_read, G - RAW_SLOTS + 1)
                dst = raw[:, slot, 0:cnt * width].rearrange("p (c n) -> p c n", c=cnt)
                sp.dma_start(dst, src.rearrange("(c p) n -> p c n", p=P)).then_inc(raw_landed[slot], 16)
            for t in range(TOK):
                sp.wait_ge(S.final_ready, t + 1)
                sp.dma_start(io["out"][0, t * P:(t + 1) * P], fout[:, t]).then_inc(S.out_stored, 16)
            sp.wait_ge(S.out_stored, 16 * TOK)

        @block.gpsimd
        def _(pool):
            n = Tally()

            def rsqrt(cnt, at=0):
                pool.wait_ge(S.var_ready, n(S.var_ready))
                pool.tensor_tensor(stat[:, 8 + at:8 + at + cnt], stat[:, at:at + cnt], minus_half[:, 0:cnt], ALU.pow
                                   ).then_inc(S.rstd_ready, 1)

            pool.memset(minus_half[:], -0.5).then_inc(S.pool_step, 1)
            pool.wait_ge(S.pool_step, 1)
            for dst, src in ((cols2[:], io["cols2"]), (stat[:, 32:34].bitcast(I32), io["positions"]),
                             (sinks[:], io["swa_sinks"].partition_broadcast(P)),
                             (gnorm[:], io["gla_norm_g"].partition_broadcast(P)),
                             (gup[:], io["gla_w_gate_up"].rearrange("l r n -> r l n")),
                             (levels[:], io["levels"].rearrange("p (l n) -> p l n", n=P))):
                pool.dma_start(dst, src).then_inc(S.small_landed, 16)
            for l in range(DEPTH):
                if l:
                    pool.wait_ge(S.x_ready, 4 * l)
                pool.dma_start(sgw[:], io["sg_w"][l].rearrange("g t s -> t g s")).then_inc(S.rows_landed, 16)
                pool.dma_start(sgln[:, 0], io["sg_ln_g"][l].partition_broadcast(P)).then_inc(S.rows_landed, 16)
                pool.dma_start(sgln[:, 1], io["sg_ln_b"][l].partition_broadcast(P)).then_inc(S.rows_landed, 16)
                rsqrt(2)
                rsqrt(2)
                for lev in range(1, LEVELS + 2):
                    pool.wait_ge(S.gla_q, n(S.gla_q))
                    pool.tensor_tensor(klev[:, lev % 2], glf[:, lev % 2], gq[:, 1], ALU.mult).then_inc(S.gla_k, 1)
                rsqrt(8)
                rsqrt(2)
            r = io["rel"]
            for l in range(DEPTH):
                x_complete(pool, l, 0)
                pool.dma_start(lam4[:], io["lambdas"][l].partition_broadcast(P)).then_inc(S.rows_landed, 16)
                pool.dma_start(bias_d[:], io["diff_bias"].rearrange("p (h k) -> p h k", h=4)).then_inc(S.rows_landed, 16)
                rsqrt(2)
                rsqrt(4, 4)
                pool.wait_ge(S.mla_done, l + 1)
                pool.dma_start(bias_c[:], bass.AP(tensor=r.tensor, offset=l * 4 * REL_PAD + 1,
                                                  ap=[[1, P], [REL_PAD, 4], [1, 2 * P]])).then_inc(S.rows_landed, 16)
                pool.dma_start(subln[:], io["diff_subln_2"][l].partition_broadcast(P)).then_inc(S.rows_landed, 16)
                rsqrt(8)
                rsqrt(2)
            pool.wait_ge(S.dve_evacuated, jobs["down11"].E + 4)
            pool.dma_start(frow[:], io["final_norm_2"].partition_broadcast(P)).then_inc(S.rows_landed, 16)
            rsqrt(2)

        @block.scalar
        def _(act):
            n = Tally()

            def link(ins):
                ins.then_inc(S.act_step, 1)
                act.wait_ge(S.act_step, n(S.act_step))

            def hi(job, j, L):
                G = group_at[L]
                act.wait_ge(raw_landed[G % RAW_SLOTS], 16 * (G // RAW_SLOTS + 1))
                if L >= SPLIT_SLOTS:
                    act.wait_ge(S.group_multiplied, L - SPLIT_SLOTS + 1)
                w = job.groups[j][1] * job.width
                act.activation(w_hi[:, L % SPLIT_SLOTS, 0:w], raw[:, G % RAW_SLOTS, 0:w], ACT.Copy
                               ).then_inc(S.hi_ready, 1)

            def evacuate(job, i):
                act.wait_ge(S.group_multiplied, tile_multiplied(job, i))
                kind, l = job.kind, job.layer
                if kind == "up":
                    h = int(job.name[-1])
                    if h == 0 and i == 0:
                        act.wait_ge(S.rstd_ready, rstd_value(l, 3))
                    done = 2 * job.tiles * (2 * l + h)
                    if i >= 2 or done:
                        act.wait_ge(S.uT_ready, done + 2 * max(i - 1, 0))
                    for t in range(TOK):
                        a = act.activation(u_nat[:, i % 2, t], ps[:, bank(job, i, t)], ACT.Relu, scale=stat[:, 8 + t:9 + t])
                        a.then_inc(S.act_evacuated if t else S.act_step, 1)
                    act.wait_ge(S.act_step, n(S.act_step))
                    act.wait_ge(S.act_evacuated, job.E + i + 1)
                    u = u_nat[:, i % 2].rearrange("p t n -> p (t n)")
                    act.activation(u, u, ACT.Square).then_inc(S.u_ready, 1)
                    return
                if kind in ("in", "rest"):
                    c0, c1 = job.col0 + i * job.width, job.col0 + (i + 1) * job.width
                    pieces = [(max(c0, a), min(c1, b), g) for a, b, g in ((0, C_SU, False), (C_SU, C_CQ, True), (C_CQ, C_Z, False))
                              if max(c0, a) < min(c1, b)]
                    pieces = [(t, *piece) for t in range(TOK) for piece in pieces]
                    for k, (t, a, b, g) in enumerate(pieces):
                        ins = act.activation(proj[:, t, a:b], ps[:, bank(job, i, t), a - c0:b - c0],
                                             ACT.Gelu_apprx_tanh if g else ACT.Copy)
                        if k < len(pieces) - 1:
                            link(ins)
                    ins.then_inc(S.act_evacuated, 1)
                    return
                for t in range(TOK):
                    src = ps[:, bank(job, i, t), 0:job.width]
                    c = job.col0 + i * job.width
                    f, scale = ACT.Copy, 1.0
                    if kind == "z":
                        dst, f = proj[:, t, c:c + job.width], ACT.Silu
                    elif kind == "out":
                        dst = out_sb[:, t, c:c + job.width]
                        link(act.activation(probs[:, t], src, ACT.Square, accum_out=stat[:, 16 + 4 * t + i:17 + 4 * t + i]))
                    elif kind == "uq":
                        dst, scale = qm[:, t, c:c + job.width], stat[:, 12 + t:13 + t]
                    elif kind == "ukv":
                        dst, scale = kv[:, t, c:c + job.width], stat[:, 14 + t:15 + t]
                    else:
                        if kind == "c2" and i == 0:
                            act.wait_ge(S.rstd_ready, rstd_value(l, 0))
                        dst, scale = proj2[:, t, c:c + job.width], stat[:, 8 + t:9 + t]
                    a = act.activation(dst, src, f, scale=scale)
                    a.then_inc(S.act_evacuated if t else S.act_step, 1)
                n(S.act_step)

            def split_bank(dst, b, scale=None, bias=None):
                act.wait_ge(S.act_bank_filled, n(S.act_bank_filled))
                u = n(S.lhs_hi) - 1
                if u >= 2:
                    act.wait_ge(S.lhs_ready, u - 1)
                src = ps[:, 6 + (n.so_far(S.act_bank_filled) - 1) % 2]
                if scale is None:
                    act.activation(hf[:, u % 2].rearrange("p c n -> p (c n)"), src, ACT.Copy).then_inc(S.act_bank_drained, 1)
                    act.wait_ge(S.act_bank_drained, n.so_far(S.act_bank_filled))
                else:
                    for c in range(2):
                        k = 2 * b + c
                        kw = {"bias": bias[:, k:k + 1]} if bias is not None else {}
                        a = act.activation(hf[:, u % 2, c], src[:, c * 2 * P:(c + 1) * 2 * P],
                                           ACT.Identity if kw else ACT.Copy, scale=scale[:, k:k + 1], **kw)
                        a.then_inc(S.act_bank_drained if c else S.act_step, 1)
                    act.wait_ge(S.act_step, n(S.act_step))
                    act.wait_ge(S.act_bank_drained, n.so_far(S.act_bank_filled))
                act.activation(dst[:, 2 * b:2 * b + 2].rearrange("p c n -> p (c n)"),
                               hf[:, u % 2].rearrange("p c n -> p (c n)"), ACT.Copy).then_inc(S.lhs_hi, 1)

            def square_sums(i, src, junk):
                for t in range(TOK):
                    act.activation(junk, src[:, t, i * COLS:(i + 1) * COLS], ACT.Square,
                                   accum_out=stat[:, 16 + 4 * t + i:17 + 4 * t + i]).then_inc(S.squares_ready, 1)
                    act.wait_ge(S.squares_ready, n(S.squares_ready))

            def squares_of(job, i, junk):
                act.wait_ge(S.dve_evacuated, job.E + i + 1)
                square_sums(i, x, junk)

            def wide(jobs_, lead=None, junk=None):
                first, prev = jobs_[0], None
                for job, i, j, L, splits in ahead(jobs_):
                    if lead and job is first and i == 0:
                        at = job.lhs0 // 2
                        if j == 0:
                            split_bank(lead[0], at, *lead[1:])
                    for group in splits[:1]:
                        hi(*group)
                    if lead and job is first and i == 0 and j + 1 < len(job.groups):
                        split_bank(lead[0], at + j + 1, *lead[1:])
                    for group in splits[1:]:
                        hi(*group)
                    last = len(job.groups) - 1
                    if j == min(1, last) and prev:
                        evacuate(*prev)
                    if junk is not None and job is jobs_[-1] and i and j == min(3, last):
                        squares_of(job, i - 1, junk)
                    if j == last:
                        prev = (job, i) if job.evac == "act" else None
                    yield
                if prev:
                    evacuate(*prev)
                yield

            def bank_copy(dst, width=COLS, scale=1.0):
                act.wait_ge(S.act_bank_filled, n(S.act_bank_filled))
                b = 6 + (n.so_far(S.act_bank_filled) - 1) % 2
                act.activation(dst, ps[0:dst.shape[0], b, 0:width], ACT.Copy, scale=scale).then_inc(S.act_bank_drained, 1)

            def attention(m):
                for i, (dst, sources, rows) in enumerate(m.prep):
                    bank_copy(dst, len(sources) * P)
                    if i % 2 or i == len(m.prep) - 1:
                        yield
                for s in range(len(m.groups) + 2):
                    if 1 <= s <= len(m.groups):
                        bank_copy(m.probsT[:, (s - 1) % 2])
                    if s < len(m.groups):
                        t, hs = m.groups[s]
                        nk, r = (t + 1) * P, s % 3
                        act.wait_ge(S.neg_max_ready, n(S.neg_max_ready))
                        for j in range(len(hs)):
                            e = m.probs[:, s % 2, j * nk:(j + 1) * nk]
                            a = act.activation(e, e, ACT.Exp, bias=smax[:, r, j:j + 1], accum_out=ssum[:, r, j:j + 1])
                            if m is swa or j < len(hs) - 1:
                                link(a)
                        if m is swa:
                            a = act.activation(ses[:, r, 0:len(hs)], ses[:, r, 0:len(hs)], ACT.Exp)
                        a.then_inc(S.probs_ready, 1)
                    yield

            f = lambda ap: ap.rearrange("p k n -> p (k n)")

            def gla(l):
                bank_copy(cgT[:], 2 * P)
                bank_copy(gq[:, 0].rearrange("p k n -> p (k n)"), scale=GDK ** -0.5)
                yield
                bank_copy(gq[:, 1].rearrange("p k n -> p (k n)"))
                act.wait_ge(S.gla_logits, l + 1)
                link(act.activation(f(gle[:, 0]), f(gle[:, 0]), ACT.Exp, scale=-1.0))
                act.activation(f(gle[:, 0]), f(gle[:, 0]), ACT.Ln, bias=K["ones"][:, 0:1]).then_inc(S.gla_ln, 1)
                yield
                yield
                for lev in range(1, LEVELS + 2):
                    act.wait_ge(S.gla_dist, n(S.gla_dist))
                    if lev >= 3:
                        act.wait_ge(S.gla_k, l * (LEVELS + 1) + lev - 2)
                    link(act.activation(f(gle[:, lev % 2]), f(gle[:, lev % 2]), ACT.Abs))
                    act.activation(f(glf[:, lev % 2]), f(gle[:, lev % 2]), ACT.Exp, scale=-1.0 / 16).then_inc(S.gla_factor, 1)
                    yield
                for _ in range(3):
                    yield

            def mixers1(l):
                yield
                yield from attention(swa)
                for _ in range(3):
                    yield
                yield from gla(l)

            def mla_steps(l):
                act.wait_ge(S.lam_in, l + 1)
                act.activation(stat[:, 48:50], stat[:, 48:50], ACT.Exp).then_inc(S.lam_exp, 1)
                yield
                yield from attention(mla)

            def dif_steps():
                yield from attention(dif)
                yield
                yield

            def chk_steps():
                yield
                yield from attention(chk)

            act.wait_ge(S.const_landed, 48)
            link(act.activation(c_col[:], c_col[:], ACT.Silu))
            act.wait_ge(S.tables, 1)
            act.activation(cs1[:].rearrange("p a t n -> p (a t n)"), cs1[:].rearrange("p a t n -> p (a t n)"), ACT.Sin
                           ).then_inc(S.ang_ready, 1)
            act.wait_ge(S.x_landed, 16)
            for l in range(DEPTH):
                for i in range(D // COLS):
                    if l:
                        act.wait_ge(S.x_ready, 4 * (l - 1) + i + 1)
                    square_sums(i, x, probs[:, 0])
                act.wait_ge(S.hcol_ready, l + 1)
                a, b, z, o = (jobs[f"{name}{l}"] for name in ("in", "rest", "z", "out"))
                steps = wide([a, b, z], (hT_hi, hcol, mod[:, l]))
                take(steps, count([a]) - 1 + 2)
                interleave(steps, count([b, z]) - 2, mixers1(l), MIX1_SLOTS)
                finish(steps)
                finish(wide([o], (hT_hi,)))
            for l in range(DEPTH):
                if l == 0:
                    act.wait_ge(S.small_landed, 16 * 6)
                a, b, q, k, r = (jobs[f"{name}{l}"] for name in ("c2", "in2", "uq", "ukv", "rest2"))
                steps = wide([a, b], (hT_hi, cols2[:, l, 0:KC]))
                take(steps, 2)
                if l == 0:
                    for i in range(D // COLS):
                        act.wait_ge(S.x_ready, 4 * (DEPTH - 1) + i + 1)
                        square_sums(i, x, probs2[:, 0])
                else:
                    squares_of(jobs[f"down{l - 1}1"], 3, probs2[:, 0])
                take(steps, count([a]) - 1)
                act.wait_ge(S.act_step, n.so_far(S.act_step))
                act.wait_ge(S.act_evacuated, a.E + 2)
                for j, (t, c0, c1) in enumerate(((0, C_CQ2, C_CKV), (1, C_CQ2, C_CKV), (0, C_CKV, C_KR), (1, C_CKV, C_KR))):
                    act.activation(kv[:, 0, 0:c1 - c0], proj2[:, t, c0:c1], ACT.Square, accum_out=stat[:, 4 + j:5 + j]
                                   ).then_inc(S.squares_ready, 1)
                    act.wait_ge(S.squares_ready, n(S.squares_ready))
                finish(steps)
                act.wait_ge(S.rstd_ready, rstd_value(l, 1))
                finish(wide([q, k], (cT_hi, cols2[:, l, 32:36])))
                steps = wide([r])
                interleave(steps, count([r]), mla_steps(l), 1 + mla.slots())
                finish(steps)
                oa, ob, oc_ = (jobs[f"{name}{l}"] for name in ("oa", "ob", "oc"))
                interleave(wide([oa], (hT_hi,)), count([oa]), dif_steps(), dif.slots() + 2)
                interleave(wide([ob], (hT_hi,)), count([ob]), chk_steps(), 1 + chk.slots())
                finish(wide([oc_], (hT_hi,), junk=probs2[:, 0]))
                steps = wide([jobs[f"{name}{l}{h}"] for h in range(2) for name in ("up", "down")],
                             (hT_hi, cols2[:, l, KC:2 * KC]), junk=junk_m[:])
                take(steps, 2)
                squares_of(oc_, 3, probs2[:, 0])
                finish(steps)
            squares_of(jobs["down11"], 3, junk_m[:])

        @block.vector
        def _(dve):
            n = Tally()

            def link(ins):
                ins.then_inc(S.dve_step, 1)
                dve.wait_ge(S.dve_step, n(S.dve_step))

            def lo(job, j, L):
                dve.wait_ge(S.hi_ready, L + 1)
                w, s = job.groups[j][1] * job.width, L % SPLIT_SLOTS
                dve.tensor_tensor(w_lo[:, s, 0:w], raw[:, group_at[L] % RAW_SLOTS, 0:w], w_hi[:, s, 0:w].bitcast(F32),
                                  ALU.subtract).then_inc(S.group_read, 1)

            def evacuate(job, i):
                dve.wait_ge(S.group_multiplied, tile_multiplied(job, i))
                if job.E + i:
                    dve.wait_ge(S.dve_evacuated, job.E + i)
                for t in range(TOK):
                    v = x[:, t, i * COLS:(i + 1) * COLS]
                    a = dve.tensor_tensor(v, v, ps[:, bank(job, i, t)], ALU.add)
                    if t == 0:
                        link(a)
                a.then_inc(S.dve_evacuated, 1)

            def dve_bank():
                u = n(S.dve_bank_filled)
                dve.wait_ge(S.dve_bank_filled, u)
                return 4 + (u - 1) % 2

            def drained(ins):
                ins.then_inc(S.dve_bank_drained, 1)
                dve.wait_ge(S.dve_bank_drained, n(S.dve_bank_drained))

            def mod_product(l, t, g, G):
                dve.wait_ge(raw_landed[G % RAW_SLOTS], 16 * (G // RAW_SLOTS + 1))
                if G:
                    dve.wait_ge(S.group_read, G)
                for a in range(2):
                    w = raw[:, G % RAW_SLOTS, a * COLS:(a + 1) * COLS]
                    c = c_col[:, 2 * g + a:2 * g + a + 1]
                    s = acc[:, t % 2, a]
                    if g == 0:
                        m = dve.tensor_scalar(s, w, c, None, ALU.mult)
                    else:
                        m = dve.scalar_tensor_tensor(out=s, in0=w, scalar=c, in1=s, op0=ALU.mult, op1=ALU.add)
                m.then_inc(S.group_read, 1)
                if g == MOD_GROUPS - 1:
                    dve.wait_ge(S.group_read, G + 1)
                    s = acc[:, t % 2]
                    dve.tensor_tensor(s[:, 0], s[:, 0], s[:, 1], ALU.add).then_inc(S.mod_ready, 1)

            def mod_out(l, t):
                b = dve_bank()
                drained(dve.tensor_tensor(mod[:, l, 4 * t:4 * t + 4], ps[:, b, 0:4],
                                          cols1[:, l, 16 + 4 * t:20 + 4 * t], ALU.add))

            def wide(jobs_, lead=None):
                first, prev = jobs_[0], None
                for job, i, j, L, splits in ahead(jobs_):
                    for m in mods_at.get(L, ()):
                        mod_product(*m)
                    if lead and job is first and i == 0:
                        at = job.lhs0 // 2
                        if j == 0:
                            split_bank(*lead, at)
                    for group in splits[:1]:
                        lo(*group)
                    if lead and job is first and i == 0 and j + 1 < len(job.groups):
                        split_bank(*lead, at + j + 1)
                    for group in splits[1:]:
                        lo(*group)
                    if L in mod_sums:
                        mod_out(*mod_sums[L])
                    last = len(job.groups) - 1
                    if j == min(1, last) and prev:
                        evacuate(*prev)
                    if job.kind == "up" and i and j == 7:
                        turned(i - 1)
                    if job.kind == "down" and i == 0 and j == 7:
                        turned(UPC // COLS - 1)
                    if j == last:
                        prev = (job, i) if job.evac == "dve" else None
                    yield
                if prev:
                    evacuate(*prev)
                yield

            def split_bank(dst_hi, dst_lo, b):
                dve.wait_ge(S.lhs_hi, n(S.lhs_hi))
                u = n.so_far(S.lhs_hi) - 1
                f = lambda ap: ap.rearrange("p c n -> p (c n)")
                dve.tensor_tensor(f(dst_lo[:, 2 * b:2 * b + 2]), f(hf[:, u % 2]),
                                  f(dst_hi[:, 2 * b:2 * b + 2]).bitcast(F32), ALU.subtract).then_inc(S.lhs_ready, 1)

            def turned(i):
                for half in range(2):
                    b = dve_bank()
                    k = slice(4 * i + 2 * half, 4 * i + 2 * half + 2)
                    h_, l_ = (u[:, k].rearrange("p c n -> p (c n)") for u in (uT_hi, uT_lo))
                    dve.tensor_scalar(h_, ps[:, b], 1.0, None, ALU.mult).then_inc(S.uT_ready, 1)
                    dve.wait_ge(S.uT_ready, n(S.uT_ready))
                    drained(dve.tensor_tensor(l_, ps[:, b], h_.bitcast(F32), ALU.subtract))

            def variance(parts):
                for j, (a, b, width) in enumerate(parts):
                    v = dve.tensor_scalar(stat[:, a:b], stat[:, a:b], 1.0 / width, EPS, ALU.mult, ALU.add)
                    if j < len(parts) - 1:
                        link(v)
                v.then_inc(S.var_ready, 1)
                n(S.var_ready)

            def x_variance():
                dve.wait_ge(S.squares_ready, n(S.squares_ready, 2 * D // COLS))
                sum_tiles()

            def sum_tiles():
                link(dve.tensor_reduce(stat[:, 0:2], stat[:, 16:24].rearrange("p (t n) -> p t n", t=TOK), AX.X, ALU.add))
                variance([(0, 2, D)])

            def rstd():
                dve.wait_ge(S.rstd_ready, n.so_far(S.var_ready))

            def rotate(heads_at, cos, sin, half, tmp):
                t1, t2 = heads_at(0, half), heads_at(half, 2 * half)
                a, b, c, d = tmp
                dve.tensor_tensor(a, t1, cos, ALU.mult)
                dve.tensor_tensor(b, t2, sin, ALU.mult)
                dve.tensor_tensor(c, t2, cos, ALU.mult)
                link(dve.tensor_tensor(d, t1, sin, ALU.mult))
                dve.tensor_tensor(t1, a, b, ALU.subtract)
                return dve.tensor_tensor(t2, c, d, ALU.add)

            def attention(m, l):
                for i in range((len(m.prep) + 1) // 2):
                    yield
                for s_ in range(len(m.groups) + 2):
                    if s_ < len(m.groups):
                        softmax(m, l, s_)
                    if s_ >= 2:
                        out(m, s_ - 2)
                    yield

            def softmax(m, l, g):
                t, hs = m.groups[g]
                nk, nh, r = (t + 1) * P, len(hs), g % 3
                b = dve_bank()
                s = ps[:, b].rearrange("p (h k) -> p h k", h=nh)
                e = m.probs[:, g % 2].rearrange("p (h k) -> p h k", h=nh)
                masks = m.masks(t, hs)
                for j0, j1, mask in masks:
                    a = dve.scalar_tensor_tensor(out=e[:, j0:j1], in0=s[:, j0:j1], scalar=m.scale, in1=mask,
                                                 op0=ALU.mult, op1=ALU.add)
                    if j1 < nh:
                        link(a)
                drained(a)
                a = dve.tensor_reduce(smax[:, r, 0:nh], e, AX.X, ALU.max, negate=True)
                if m is swa:
                    link(a)
                    k = slice(hs[0], hs[-1] + 1, 2)
                    link(dve.tensor_tensor(smax[:, r, 0:nh], smax[:, r, 0:nh], neg_sinks[:, l, k], ALU.min))
                    a = dve.tensor_tensor(ses[:, r, 0:nh], smax[:, r, 0:nh], sinks[:, l, k], ALU.add)
                a.then_inc(S.neg_max_ready, 1)

            def out(m, g):
                t, hs = m.groups[g]
                nh, r = len(hs), g % 3
                b = dve_bank()
                den, rec = ssum[:, r, 0:nh], srec[:, r, 0:nh]
                if m is swa:
                    den = sden[:, r, 0:nh]
                    link(dve.tensor_tensor(den, ssum[:, r, 0:nh], ses[:, r, 0:nh], ALU.add))
                link(dve.reciprocal(rec, den))
                o = ps[:, b, 0:nh * m.dv].rearrange("p (h d) -> p h d", h=nh)
                if m is not dif:
                    drained(dve.tensor_tensor(m.out(t, hs), o, spread(rec, m.dv), ALU.mult))
                    return
                link(dve.tensor_scalar(sden[:, r, 0:nh], rec, stat[:, 52:53], None, ALU.mult))
                for j in range(0, nh, 2):
                    link(dve.tensor_scalar(dtmp[:, 0], o[:, j + 1], sden[:, r, j + 1:j + 2], None, ALU.mult))
                    a = dve.scalar_tensor_tensor(out=m.out(t, hs[j]), in0=o[:, j], scalar=rec[:, j:j + 1],
                                                 in1=dtmp[:, 0], op0=ALU.mult, op1=ALU.subtract)
                    if j + 2 < nh:
                        link(a)
                drained(a)

            def rotation1(l):
                dve.wait_ge(S.act_evacuated, jobs[f"in{l}"].E + 3)
                heads = QH + KVH
                tmp = [v.rearrange("p (h n) -> p h n", h=heads) for v in rotation_tmp]
                for t in range(TOK):
                    qk = proj[:, t, 0:heads * HD].rearrange("p (h d) -> p h d", d=HD)
                    cos, sin = repeat(cs1[:, 0, t], heads), repeat(cs1[:, 1, t], heads)
                    link(rotate(lambda a, b: qk[:, :, a:b], cos, sin, HALF, tmp))
                for t in range(TOK):
                    k = proj[:, t, C_K:C_V].rearrange("p (h d) -> p h d", d=HD).unsqueeze(2).broadcast_to([P, KVH, 2, HD])
                    r = dve.tensor_copy(keys2[t].rearrange("p (h a d) -> p h a d", h=KVH, a=2), k)
                r.then_inc(S.rotated, 1)
                yield

            def spatial(l):
                v = proj[:, :, C_SV:C_SV + COLS]
                dve.wait_ge(S.act_evacuated, jobs[f"rest{l}"].E + 3)
                for t in range(TOK):
                    link(dve.bn_stats(bn[:, t], v[:, t]))
                    link(dve.bn_aggr(stat[:, 24 + 2 * t:26 + 2 * t], bn[:, t]))
                    a = dve.tensor_scalar(stat[:, t:t + 1], stat[:, 25 + 2 * t:26 + 2 * t], EPS, None, ALU.add)
                    if t == 0:
                        link(a)
                a.then_inc(S.var_ready, 1)
                n(S.var_ready)
                for half in range(2):
                    b = dve_bank()
                    drained(dve.tensor_tensor(sgwT[:, 4 * half:4 * half + 4], ps[:, b].rearrange("p (g t) -> p g t", g=4),
                                              repeat(K["tril"], 4), ALU.mult))
                yield
                rstd()
                dve.wait_ge(S.rows_landed, rows_value(1, l))
                for t in range(TOK):
                    link(dve.tensor_scalar(v[:, t], v[:, t], stat[:, 24 + 2 * t:25 + 2 * t], stat[:, 8 + t:9 + t],
                                           ALU.subtract, ALU.mult))
                    link(dve.tensor_tensor(v[:, t], v[:, t], sgln[:, 0], ALU.mult))
                    a = dve.tensor_tensor(v[:, t], v[:, t], sgln[:, 1], ALU.add)
                    a.then_inc(S.v_ready, 1)
                yield
                for half in range(2):
                    b = dve_bank()
                    for j in range(4):
                        g = 4 * half + j
                        u = proj[:, :, C_SU + g * SGD:C_SU + (g + 1) * SGD]
                        a = dve.scalar_tensor_tensor(out=u, in0=ps[:, b, j * P:(j + 1) * P].rearrange("p (n c) -> p n c", n=TOK),
                                                     scalar=cols1[:, l, 64 + g:65 + g], in1=u, op0=ALU.add, op1=ALU.mult)
                        if j < 3:
                            link(a)
                    drained(a)
                yield

            def dist(lev):
                e = gle[:, lev % 2]
                if lev <= LEVELS:
                    n_b = 2 ** lev
                    g = glb[:].rearrange("p k (b n) -> p (k b) n", n=n_b)
                    mid = g[:, :, n_b // 2 - 1:n_b // 2].broadcast_to([P, 4 * P // n_b, n_b])
                    dve.tensor_tensor(e.rearrange("p k (b n) -> p (k b) n", n=n_b), g, mid, ALU.subtract
                                      ).then_inc(S.gla_dist, 1)
                else:
                    link(dve.tensor_tensor(e[:, :, 0:P], glb[:, :, 0:P],
                                           glb[:, :, P - 1:P].broadcast_to([P, 2, P]), ALU.subtract))
                    dve.tensor_copy(e[:, :, P:2 * P], glb[:, :, P:2 * P]).then_inc(S.gla_dist, 1)

            def consume(lev):
                for t in range(TOK if lev <= LEVELS else 1):
                    b = dve_bank()
                    if lev <= LEVELS:
                        drained(dve.copy_predicated(pairs[:, t].rearrange("p (h n) -> p h n", h=GH),
                                                    repeat(levels[:, lev], GH),
                                                    ps[:, b].rearrange("p (h n) -> p h n", h=GH)))
                    else:
                        drained(dve.tensor_copy(pairs[:, 2], ps[:, b]))

            def gla(l):
                yield
                b = dve_bank()
                link(dve.tensor_scalar(glx[:, 0], ps[:, b, 0:2 * P], cols1[:, l, 72:73], None, ALU.add))
                drained(dve.tensor_scalar(glx[:, 1], ps[:, b, 2 * P:4 * P], cols1[:, l, 73:74], None, ALU.add))
                dve.scalar_tensor_tensor(out=gle[:, 0], in0=glx[:], scalar=-1.0, in1=glx[:], op0=ALU.mult, op1=ALU.max
                                         ).then_inc(S.gla_logits, 1)
                link(dve.memset(pairs[:, 0:2], 0.0))
                yield
                dve.wait_ge(S.gla_ln, l + 1)
                link(dve.scalar_tensor_tensor(out=glx[:], in0=glx[:], scalar=0.0, in1=gle[:, 0], op0=ALU.min, op1=ALU.subtract))
                for kt in range(2):
                    for t in range(TOK):
                        s = slice(t * P, (t + 1) * P)
                        link(dve.tensor_tensor_scan(glb[:, kt, s], K["ones"], glx[:, kt, s], 0.0, ALU.mult, ALU.add))
                dist(1)
                dist(2)
                consume(0)
                yield
                for lev in range(1, LEVELS + 2):
                    dve.wait_ge(S.gla_factor, n(S.gla_factor))
                    dve.tensor_tensor(qlev[:, lev % 2], glf[:, lev % 2], gq[:, 0], ALU.mult).then_inc(S.gla_q, 1)
                    if lev + 2 <= LEVELS + 1:
                        dist(lev + 2)
                    if lev >= 2:
                        consume(lev - 1)
                    yield
                consume(LEVELS + 1)
                yield
                for t in range(TOK):
                    b = dve_bank()
                    drained(dve.tensor_copy(oc[:, t * COLS:(t + 1) * COLS], ps[:, b]))
                link(dve.tensor_tensor(osq, oc, oc, ALU.mult))
                link(dve.tensor_reduce(stat[:, 0:8], osq.rearrange("p (h d) -> p h d", h=8), AX.X, ALU.add))
                variance([(0, 8, GDV)])
                yield
                rstd()
                for t in range(TOK):
                    y = proj[:, t, C_CV:C_CV + COLS].rearrange("p (h d) -> p h d", h=GH)
                    link(dve.tensor_tensor(y, oc[:, t * COLS:(t + 1) * COLS].rearrange("p (h d) -> p h d", h=GH),
                                           spread(stat[:, 8 + 4 * t:12 + 4 * t], GDV), ALU.mult))
                    link(dve.tensor_tensor(y, y, repeat(gnorm[:, l], GH), ALU.mult))
                yield

            def mixers1(l):
                yield from rotation1(l)
                yield from attention(swa, l)
                yield from spatial(l)
                yield from gla(l)

            def mla_steps(l):
                dve.wait_ge(S.rows_landed, rows_value(2, l, "first"))
                link(dve.tensor_tensor(lamt[:], lam4[:, 0:2], lam4[:, 2:4], ALU.mult))
                dve.tensor_reduce(stat[:, 48:50], lamt[:], AX.X, ALU.add).then_inc(S.lam_in, 1)
                dve.wait_ge(S.act_evacuated, jobs[f"ukv{l}"].E + 4)
                tmp = [rt[:, i // 2, (i % 2) * 2 * P:(i % 2 + 1) * 2 * P] for i in range(4)]
                for t in range(TOK):
                    q = qm[:, t].rearrange("p (h d) -> p h d", h=HA)
                    cos, sin = K["cos2"][:, 32 * t:32 * t + 32], K["sin2"][:, 32 * t:32 * t + 32]
                    link(rotate(lambda a, b: q[:, :, NOPE + a:NOPE + b], repeat(cos, HA), repeat(sin, HA), 32,
                                [v.rearrange("p (h n) -> p h n", h=HA) for v in tmp]))
                    a = rotate(lambda a, b: proj2[:, t, C_KR + a:C_KR + b], cos, sin, 32, [v[:, 0:32] for v in tmp])
                    if t == 0:
                        link(a)
                a.then_inc(S.rotated, 1)
                yield
                yield from attention(mla, l)

            def dif_steps(l, lam_init):
                yield from attention(dif, l)
                yd = [proj2[:, t, C_QB:C_QB + 4 * P].rearrange("p (h d) -> p h d", h=4) for t in range(TOK)]
                for t in range(TOK):
                    sq = probs2[:, t].rearrange("p (h d) -> p h d", h=4)
                    link(dve.tensor_tensor(sq, yd[t], yd[t], ALU.mult))
                    link(dve.tensor_reduce(stat[:, 4 * t:4 * t + 4], sq, AX.X, ALU.add))
                variance([(0, 8, P)])
                yield
                rstd()
                dve.wait_ge(S.rows_landed, rows_value(2, l))
                for t in range(TOK):
                    link(dve.tensor_tensor(yd[t], yd[t], spread(stat[:, 8 + 4 * t:12 + 4 * t], P), ALU.mult))
                    dve.scalar_tensor_tensor(out=yd[t], in0=yd[t], scalar=1.0 - lam_init, in1=repeat(subln[:], 4),
                                             op0=ALU.mult, op1=ALU.mult).then_inc(S.yd_ready, 1)
                yield

            def chk_steps(l):
                for half in range(2):
                    b = dve_bank()
                    drained(dve.tensor_tensor(bias_c[:, 2 * half:2 * half + 2], ps[:, b].rearrange("p (h k) -> p h k", h=2),
                                              repeat(K["chunk"], 2), ALU.add))
                yield
                yield from attention(chk, l)

            dve.wait_ge(S.const_landed, 48)
            dve.wait_ge(S.small_landed, 16 * 6)
            link(dve.tensor_copy(stat[:, 34:36], stat[:, 32:34].bitcast(I32)))
            for t in range(TOK):
                link(dve.tensor_scalar(cs1[:, 1, t], K["inv_freq"], stat[:, 34 + t:35 + t], None, ALU.mult))
            ang, turn = cs1[:, 1].rearrange("p t n -> p (t n)"), turns[:]
            for part, quarter in ((0, 0.25), (1, 0.0)):
                r = cs1[:, part].rearrange("p t n -> p (t n)")
                link(dve.tensor_scalar(turn, ang, 1.0 / (2 * np.pi), quarter, ALU.mult, ALU.add))
                link(dve.tensor_scalar(turn, turn, ROUND, None, ALU.add))
                link(dve.tensor_scalar(turn, turn, ROUND, None, ALU.subtract))
                for j, c in enumerate(TWO_PI):
                    link(dve.scalar_tensor_tensor(out=r, in0=turn, scalar=-c, in1=ang if j == 0 else r,
                                                  op0=ALU.mult, op1=ALU.add))
                link(dve.tensor_scalar(r, r, float(np.pi / 2) if part == 0 else 0.0, None, ALU.add))
                a = dve.tensor_scalar(r, r, PI_BELOW, -PI_BELOW, ALU.min, ALU.max)
                if part == 0:
                    link(a)
            a.then_inc(S.tables, 1)
            link(dve.tensor_scalar(neg_sinks[:], sinks[:], -1.0, None, ALU.mult))
            dve.wait_ge(S.ang_ready, 1)

            for m in mods_first:
                l, t, g, G = m
                mod_product(*m)
                if g == MOD_GROUPS - 1 and t:
                    mod_out(0, t - 1)
            mod_out(0, 7)
            for l in range(DEPTH):
                dve.scalar_tensor_tensor(out=hcol[:], in0=mod[:, l, KC:2 * KC], scalar=1.0, in1=cols1[:, l, 0:KC],
                                         op0=ALU.add, op1=ALU.mult).then_inc(S.hcol_ready, 1)
                x_variance()
                rstd()
                for i in range(D // COLS):
                    for t in range(TOK):
                        k = slice(i * COLS, (i + 1) * COLS)
                        a = dve.tensor_scalar(xn[:, t, k], x[:, t, k], stat[:, 8 + t:9 + t], None, ALU.mult)
                    a.then_inc(S.xn_ready, 1)
                a, b, z, o = (jobs[f"{name}{l}"] for name in ("in", "rest", "z", "out"))
                steps = wide([a, b, z], (hT_hi, hT_lo))
                take(steps, count([a]) - 1 + 2)
                interleave(steps, count([b, z]) - 2, mixers1(l), MIX1_SLOTS)
                finish(steps)
                dve.wait_ge(S.act_evacuated, jobs[f"z{l}"].E + 4)
                for at0, c, w in ((0, C_Q, 1024), (1024, C_SU, COLS), (1536, C_CV, COLS)):
                    y = proj[:, :, C_Z + at0:C_Z + at0 + w]
                    dve.tensor_tensor(y, y, proj[:, :, c:c + w], ALU.mult).then_inc(S.y_ready, 1)

                def diagonal(i):
                    for k in range(4):
                        a = dve.tensor_scalar(diag[i % 2][:, k * P:(k + 1) * P], ident, gcol[:, 4 * i + k:4 * i + k + 1],
                                              None, ALU.mult)
                    a.then_inc(S.diag_ready, 1)
                dve.wait_ge(S.y_ready, 3 * (l + 1))
                link(dve.tensor_tensor(gcol[:], mod[:, l, 2 * KC:3 * KC], cols1[:, l, 74:90], ALU.mult))
                steps = wide([o], (hT_hi, hT_lo))
                take(steps, 8)
                diagonal(0)
                for i in range(D // COLS):
                    take(steps, 1)
                    if i + 1 < D // COLS:
                        diagonal(i + 1)
                    b = dve_bank()
                    drained(dve.tensor_copy(gp[i], ps[:, b]))

                def times_gp(i):
                    dve.wait_ge(S.act_evacuated, o.E + i + 1)
                    v = out_sb[:, :, i * COLS:(i + 1) * COLS]
                    return dve.tensor_tensor(v, v, repeat(gp[i], TOK), ALU.mult)
                for i in range(3):
                    take(steps, 8 if i else 0)
                    if i:
                        times_gp(i - 1)
                take(steps, 3)
                times_gp(2)
                finish(steps)
                link(times_gp(3))
                sum_tiles()
                rstd()
                for i in range(D // COLS):
                    k = slice(i * COLS, (i + 1) * COLS)
                    for t in range(TOK):
                        a = dve.scalar_tensor_tensor(out=x[:, t, k], in0=out_sb[:, t, k], scalar=stat[:, 8 + t:9 + t],
                                                     in1=x[:, t, k], op0=ALU.mult, op1=ALU.add)
                    a.then_inc(S.x_ready, 1)
                dve.wait_ge(S.x_ready, 4 * (l + 1))

            for l in range(DEPTH):
                lam_init = 0.8 - 0.6 * math.exp(-0.3 * l)
                a, b, q, k, r = (jobs[f"{name}{l}"] for name in ("c2", "in2", "uq", "ukv", "rest2"))
                steps = wide([a, b], (hT_hi, hT_lo))
                take(steps, 2)
                x_variance()
                take(steps, count([a]) - 1)
                dve.wait_ge(S.squares_ready, n(S.squares_ready, 4))
                variance([(4, 6, C_CKV), (6, 8, C_KR - C_CKV)])
                finish(steps)
                finish(wide([q, k], (cT_hi, cT_lo)))
                interleave(wide([r]), count([r]), mla_steps(l), 1 + mla.slots())
                dve.wait_ge(S.lam_exp, l + 1)
                a = dve.tensor_scalar(stat[:, 52:53], stat[:, 48:49], stat[:, 49:50], lam_init, ALU.subtract, ALU.add)
                a.then_inc(S.mla_done, 1)
                dve.wait_ge(S.mla_done, l + 1)
                oa, ob, oc_ = (jobs[f"{name}{l}"] for name in ("oa", "ob", "oc"))
                interleave(wide([oa], (hT_hi, hT_lo)), count([oa]), dif_steps(l, lam_init), dif.slots() + 2)
                interleave(wide([ob], (hT_hi, hT_lo)), count([ob]), chk_steps(l), 1 + chk.slots())
                finish(wide([oc_], (hT_hi, hT_lo)))
                steps = wide([jobs[f"{name}{l}{h}"] for h in range(2) for name in ("up", "down")], (hT_hi, hT_lo))
                take(steps, 2)
                x_variance()
                finish(steps)
            x_variance()
            rstd()
            dve.wait_ge(S.rows_landed, 16 * (ROWS1 * DEPTH + ROWS2 * DEPTH + 1))
            for t in range(TOK):
                dve.scalar_tensor_tensor(out=fout[:, t], in0=x[:, t], scalar=stat[:, 8 + t:9 + t], in1=frow[:],
                                         op0=ALU.mult, op1=ALU.mult).then_inc(S.final_ready, 1)

        @block.tensor
        def _(pe):
            n = Tally()

            def act_bank():
                u = n(S.act_bank_filled) - 1
                if u >= 2:
                    pe.wait_ge(S.act_bank_drained, u - 1)
                return 6 + u % 2

            def dve_bank():
                u = n(S.dve_bank_filled) - 1
                if u >= 2:
                    pe.wait_ge(S.dve_bank_drained, u - 1)
                return 4 + u % 2

            def act_done():
                pe.wait_ge(S.act_bank_drained, n.so_far(S.act_bank_filled))

            def dve_done():
                pe.wait_ge(S.dve_bank_drained, n.so_far(S.dve_bank_filled))

            def transposes(sources, rows=P):
                b = act_bank()
                for j, s in enumerate(sources):
                    mm = pe.transpose(ps[0:rows, b, j * P:(j + 1) * P], s, ident)
                mm.then_inc(S.act_bank_filled, 1)

            def multiply(job, i, j, L):
                hi, lo = job.lhs
                T = job.T + i
                if j == 0 and T >= 2:
                    before = next(b for b in order if b.T <= T - 2 < b.T + b.tiles)
                    pe.wait_ge(S.act_evacuated if before.evac == "act" else S.dve_evacuated,
                               before.E + T - 2 - before.T + 1)
                pe.wait_ge(S.group_read, group_at[L] + 1)
                s = L % SPLIT_SLOTS
                k0, cnt = job.groups[j]
                for c in range(cnt):
                    wh, wl = (w[:, s, c * job.width:(c + 1) * job.width] for w in (w_hi, w_lo))
                    k = job.lhs0 + k0 + c
                    for t in range(TOK):
                        o = ps[:, bank(job, i, t), 0:job.width]
                        a, b = (v[:, k, t * P:(t + 1) * P] for v in (hi, lo))
                        pe.matmul(o, a, wh, start=k0 + c == 0, stop=False)
                        pe.matmul(o, a, wl, start=False, stop=False)
                        mm = pe.matmul(o, b, wh, start=False, stop=k0 + c == job.chunks - 1)
                mm.then_inc(S.group_multiplied, 1)

            def mod_total(l, t):
                pe.wait_ge(S.mod_ready, n(S.mod_ready))
                b = dve_bank()
                for j in range(4):
                    mm = pe.matmul(ps[:, b, j:j + 1], acc[:, t % 2, 0, j * P:(j + 1) * P], K["ones"][:, 0:1],
                                   start=True, stop=True)
                mm.then_inc(S.dve_bank_filled, 1)

            def turn_u(i):
                pe.wait_ge(S.u_ready, n(S.u_ready))
                for c0 in (0, 2):
                    b = dve_bank()
                    for a in range(4):
                        c = c0 + a // 2
                        mm = pe.transpose(ps[:, b, a * P:(a + 1) * P], u_nat[:, i % 2, a % 2, c * P:(c + 1) * P], ident)
                    mm.then_inc(S.dve_bank_filled, 1)

            def fills(jobs_, lead=None):
                kind, l = jobs_[0].kind, jobs_[0].layer

                def turn(b):
                    if kind == "out":
                        pe.wait_ge(S.y_ready, 3 * l + (1, 1, 1, 1, 2, 2, 3, 3)[b])
                    elif kind == "in":
                        pe.wait_ge(S.xn_ready, 4 * l + b // 2 + 1)
                    elif kind == "c2" and l == 0:
                        pe.wait_ge(S.x_ready, 4 * (DEPTH - 1) + b // 2 + 1)
                    elif kind in ("c2", "up"):
                        last = jobs[f"down{l - 1}1" if kind == "c2" else f"oc{l}"]
                        pe.wait_ge(S.dve_evacuated, last.E + b // 2 + 1)
                    transposes([lead(c, t) for c in (2 * b, 2 * b + 1) for t in range(TOK)])
                for job, i, j, L in each_group(jobs_):
                    if lead and job is jobs_[0] and i == 0:
                        if j == 0:
                            turn(0)
                        if j + 1 < len(job.groups):
                            turn(j + 1)
                    if L in mod_sums:
                        mod_total(*mod_sums[L])
                    yield
                yield

            def products(jobs_, lead=False):
                for job, i, j, L in each_group(jobs_):
                    if lead and job is jobs_[0] and i == 0:
                        pe.wait_ge(S.lhs_ready, n(S.lhs_ready))
                    if (job.kind == "up" and i or job.kind == "down" and i == 0) and j == 4:
                        turn_u((i - 1) % (UPC // COLS))
                    if job.kind == "down" and i == 0 and j in (0, 14):
                        dve_done()
                    multiply(job, i, j, L)
                    yield
                yield

            def together(fill, product, k):
                for _ in range(k):
                    take(fill, 1)
                    take(product, 1)

            def interleave_pe(fill, product, total, mixer, slots):
                for k in share(total, slots):
                    take(fill, k)
                    next(mixer)
                    take(product, k)
                finish(mixer)

            def attention(m):
                for i, (dst, sources, rows) in enumerate(m.prep):
                    transposes(sources, rows)
                    if i % 2 or i == len(m.prep) - 1:
                        yield
                for s in range(len(m.groups) + 2):
                    if s < len(m.groups):
                        t, hs = m.groups[s]
                        nk = (t + 1) * P
                        if s == 0:
                            act_done()
                        b = dve_bank()
                        for j, h in enumerate(hs):
                            parts = m.qk(h)
                            for a, (q, k) in enumerate(parts):
                                mm = pe.matmul(ps[:, b, j * nk:(j + 1) * nk], q[:, t * P:(t + 1) * P], k[:, 0:nk],
                                               start=a == 0, stop=a == len(parts) - 1)
                        mm.then_inc(S.dve_bank_filled, 1)
                    copied = n.so_far(S.act_bank_filled)
                    if 1 <= s <= len(m.groups):
                        pe.wait_ge(S.probs_ready, n(S.probs_ready))
                        transposes([m.probs[:, (s - 1) % 2, j * P:(j + 1) * P] for j in range(4)])
                    if s >= 2:
                        t, hs = m.groups[s - 2]
                        b = dve_bank()
                        pe.wait_ge(S.act_bank_drained, copied)
                        for j, h in enumerate(hs):
                            for kk in range(t + 1):
                                i = j * (t + 1) + kk
                                mm = pe.matmul(ps[:, b, j * m.dv:(j + 1) * m.dv], m.probsT[:, s % 2, i * P:(i + 1) * P],
                                               m.v(h, kk), start=kk == 0, stop=kk == t)
                        mm.then_inc(S.dve_bank_filled, 1)
                    yield

            def spatial(l):
                pe.wait_ge(S.rows_landed, rows_value(1, l))
                for half in range(2):
                    b = dve_bank()
                    for j in range(4):
                        mm = pe.transpose(ps[:, b, j * P:(j + 1) * P], sgw[:, 4 * half + j], ident)
                    mm.then_inc(S.dve_bank_filled, 1)
                yield
                yield
                dve_done()
                pe.wait_ge(S.v_ready, TOK * (l + 1))
                for half in range(2):
                    b = dve_bank()
                    for j in range(4):
                        g = 4 * half + j
                        mm = pe.matmul(ps[:, b, j * P:(j + 1) * P].rearrange("p (n c) -> p n c", n=TOK), sgwT[:, g],
                                       proj[:, :, C_SV + g * SGD:C_SV + (g + 1) * SGD], start=True, stop=True)
                    mm.then_inc(S.dve_bank_filled, 1)
                yield

            def gla(l):
                pe.wait_ge(S.act_evacuated, jobs[f"rest{l}"].E + 6)
                transposes([proj[:, t, C_CG:C_CG + RANK] for t in range(TOK)], RANK)
                transposes([proj[:, t, C_CQ + kt * P:C_CQ + (kt + 1) * P] for kt in range(2) for t in range(TOK)])
                yield
                act_done()
                transposes([proj[:, t, C_CK + kt * P:C_CK + (kt + 1) * P] for kt in range(2) for t in range(TOK)])
                b = dve_bank()
                for kt in range(2):
                    mm = pe.matmul(ps[:, b, kt * 2 * P:(kt + 1) * 2 * P], gup[:, l, kt * P:(kt + 1) * P], cgT[:],
                                   start=True, stop=True)
                mm.then_inc(S.dve_bank_filled, 1)
                yield

                def level(lev):
                    q, k = gq[:, 0], gq[:, 1]
                    if lev:
                        pe.wait_ge(S.gla_q, n(S.gla_q))
                        pe.wait_ge(S.gla_k, n(S.gla_k))
                        q, k = qlev[:, lev % 2], klev[:, lev % 2]
                    for ts, tt in (((0, 0), (1, 1)) if lev <= LEVELS else ((0, 1),)):
                        b = dve_bank()
                        for h in (0, 2, 1, 3):
                            r = (h % 2) * GDK
                            if h == 1:
                                mm.then_inc(S.pe_step, 1)
                                pe.wait_ge(S.pe_step, n(S.pe_step))
                            mm = pe.matmul(ps[:, b, h * P:(h + 1) * P], k[r:r + GDK, h // 2, ts * P:(ts + 1) * P],
                                           q[r:r + GDK, h // 2, tt * P:(tt + 1) * P], start=True, stop=True)
                        mm.then_inc(S.dve_bank_filled, 1)
                act_done()
                level(0)
                yield
                yield
                for lev in range(1, LEVELS + 2):
                    level(lev)
                    yield
                dve_done()
                for t in range(TOK):
                    b = dve_bank()
                    terms = [(0, 0)] if t == 0 else [(1, 1), (2, 0)]
                    for h in range(GH):
                        for a, (i, sv) in enumerate(terms):
                            mm = pe.matmul(ps[:, b, h * P:(h + 1) * P], pairs[:, i, h * P:(h + 1) * P],
                                           proj[:, sv, C_CV + h * P:C_CV + (h + 1) * P],
                                           start=a == 0, stop=a == len(terms) - 1)
                    mm.then_inc(S.dve_bank_filled, 1)
                yield
                yield

            def mixers1(l):
                yield
                pe.wait_ge(S.rotated, n(S.rotated))
                yield from attention(swa)
                yield from spatial(l)
                yield from gla(l)

            def mla_steps():
                yield
                pe.wait_ge(S.rotated, n(S.rotated))
                yield from attention(mla)

            def dif_steps(l):
                yield from attention(dif)
                yield
                yield

            def chk_steps(l):
                pe.wait_ge(S.rows_landed, rows_value(2, l))
                for half in range(2):
                    b = dve_bank()
                    pe.matmul(ps[:, b], K["flip"], bias_c[:, 2 * half:2 * half + 2].rearrange("p h k -> p (h k)"),
                              start=True, stop=True).then_inc(S.dve_bank_filled, 1)
                yield
                yield from attention(chk)

            pe.wait_ge(S.const_landed, 48)
            pe.wait_ge(S.small_landed, 16 * 6)
            for t in range(8):
                mod_total(0, t)
            for l in range(DEPTH):
                a, b, z, o = (jobs[f"{name}{l}"] for name in ("in", "rest", "z", "out"))
                fill = fills([a, b, z], lambda c, t: xn[:, t, c * P:(c + 1) * P])
                product = products([a, b, z], lead=True)
                together(fill, product, count([a]) - 1 + 2)
                interleave_pe(fill, product, count([b, z]) - 2, mixers1(l), MIX1_SLOTS)
                finish(product)
                fill, product = fills([o], lambda c, t: proj[:, t, C_Z + c * P:C_Z + (c + 1) * P]), products([o], lead=True)
                together(fill, product, 8)
                for i in range(D // COLS):
                    take(fill, 1)
                    pe.wait_ge(S.diag_ready, n(S.diag_ready))
                    b = dve_bank()
                    pe.matmul(ps[:, b], K["ones"], diag[i % 2], start=True, stop=True).then_inc(S.dve_bank_filled, 1)
                    take(product, 1)
                together(fill, product, count([o]) - 12)
            for l in range(DEPTH):
                a, b, q, k, r = (jobs[f"{name}{l}"] for name in ("c2", "in2", "uq", "ukv", "rest2"))
                x_chunk = lambda c, t: x[:, t, c * P:(c + 1) * P]
                together(fills([a, b], x_chunk), products([a, b], lead=True), count([a, b]))
                together(fills([q, k], lambda c, t: proj2[:, t, c * P:(c + 1) * P]), products([q, k], lead=True), count([q, k]))
                interleave_pe(fills([r]), products([r]), count([r]), mla_steps(), 1 + mla.slots())
                pe.wait_ge(S.act_evacuated, r.E + r.tiles)
                dve_done()
                oa, ob, oc_ = (jobs[f"{name}{l}"] for name in ("oa", "ob", "oc"))
                interleave_pe(fills([oa], lambda c, t: y_mla[:, t, c * P:(c + 1) * P]), products([oa], lead=True), count([oa]),
                              dif_steps(l), dif.slots() + 2)
                pe.wait_ge(S.yd_ready, TOK * (l + 1))
                interleave_pe(fills([ob], lambda c, t: proj2[:, t, C_QB + c * P:C_QB + (c + 1) * P]),
                              products([ob], lead=True), count([ob]), chk_steps(l), 1 + chk.slots())
                dve_done()
                together(fills([oc_], lambda c, t: proj2[:, t, C_QC + c * P:C_QC + (c + 1) * P]),
                         products([oc_], lead=True), count([oc_]))
                mlp = [jobs[f"{name}{l}{h}"] for h in range(2) for name in ("up", "down")]
                together(fills(mlp, x_chunk), products(mlp, lead=True), count(mlp))


_INPUTS = ("x", "w_mod", "w_in", "w_out", "swa_sinks", "sg_w", "sg_ln_g", "sg_ln_b",
           "gla_w_gate_up", "gla_norm_g", "w_in_2", "w_uq_2", "w_ukv_2", "w_o_2", "w_up_2", "w_down_2",
           "diff_subln_2", "final_norm_2")


def columns(v):
    return v.reshape(v.shape[0], -1, P).transpose(2, 0, 1)


def kernel(**inputs):
    import concourse.bacc as bacc
    from concourse.bass_utils import run_bass_kernel_spmd as run

    a = {k: np.asarray(v) for k, v in inputs.items()}
    const, levels, diff = constants()
    arrays = {k: a[k] for k in _INPUTS}
    arrays["c"] = a["c"].reshape(KC, P).T
    arrays["positions"] = a["positions"].reshape(TOK, P).T
    arrays["cols1"] = np.concatenate([columns(a["g_pre"]), columns(a["b_mod"]), a["sg_b"].transpose(2, 0, 1),
                                      columns(a["gla_b_gate"]), columns(a["g_post"])], axis=2)
    arrays["cols2"] = np.concatenate([columns(a[k]) for k in ("attn_norm_2", "mlp_norm_2", "q_a_norm_2", "kv_a_norm_2")], axis=2)
    arrays["lambdas"] = np.stack([a[k] for k in ("lambda_q1_2", "lambda_q2_2", "lambda_k1_2", "lambda_k2_2")], axis=1)
    arrays["rel"] = np.concatenate([a["rel_bias_2"][:, :, ::-1],
                                    np.zeros((DEPTH, 4, REL_PAD - REL), np.float32)], axis=2)
    arrays["const"], arrays["levels"], arrays["diff_bias"] = const, levels, diff

    nc = bacc.Bacc("TRN2", target_bir_lowering=False, num_devices=1)
    io, sent = {}, {}
    for name, v in arrays.items():
        v = np.ascontiguousarray(v)
        sent[f"in_{name}"] = v
        io[name] = nc.dram_tensor(f"in_{name}", v.shape, mybir.dt.from_np(v.dtype), kind="ExternalInput").ap()
    io["out"] = nc.dram_tensor("out_0", (1, TOK * P, D), F32, kind="ExternalOutput").ap()
    build(nc, io)
    return run(nc, [sent], core_ids=[0]).results[0]["out_0"]
```
